# Optimizing a Trainium2 kernel written in Bass

```python
import math
import jax, jax.numpy as jnp
from jax import lax
import numpy as np

D_MODEL = 1024
BATCH = 1
SEQ = 256
DEPTH = 2

GRID_W = 64
CTX_LEN = 256

ATTN_HEADS = 4
ATTN_HEAD_DIM = 64
ATTN_V_DIM = 2 * ATTN_HEAD_DIM
ATTN_WIDTH = ATTN_HEADS * ATTN_V_DIM
QK_WIDTH = ATTN_HEADS * 2 * ATTN_HEAD_DIM
POOL_WINDOWS = (2, 4, 8, 16)
POOL_WIDTH = D_MODEL // 4
POOL_GROUP = POOL_WIDTH // len(POOL_WINDOWS)
CONV_WIDTH = D_MODEL // 4
CONV_KERNEL = 31
CONV_PAD = CONV_KERNEL // 2

MIX_WIDTH = ATTN_WIDTH + POOL_WIDTH + CONV_WIDTH
IN_WIDTH = 2 * QK_WIDTH + ATTN_WIDTH + POOL_WIDTH + 2 * CONV_WIDTH
SPLITS = (QK_WIDTH, 2 * QK_WIDTH, 2 * QK_WIDTH + ATTN_WIDTH,
          2 * QK_WIDTH + ATTN_WIDTH + POOL_WIDTH,
          2 * QK_WIDTH + ATTN_WIDTH + POOL_WIDTH + CONV_WIDTH)

FFN_HIDDEN = ((8 * D_MODEL + 3 * 256 - 1) // (3 * 256)) * 256
ROPE_THETA = 10000.0
EPS = 1e-6
BLOCK_Q = 128


def rms_norm(x, g):
    xf = x.astype(jnp.float32)
    y = xf * lax.rsqrt(jnp.mean(xf * xf, axis=-1, keepdims=True) + EPS)
    return (y * g.astype(jnp.float32)).astype(x.dtype)

def layer_norm(x, g, b):
    xf = x.astype(jnp.float32)
    mu = jnp.mean(xf, axis=-1, keepdims=True)
    var = jnp.mean(jnp.square(xf - mu), axis=-1, keepdims=True)
    y = (xf - mu) * lax.rsqrt(var + EPS)
    return (y * g.astype(jnp.float32) + b.astype(jnp.float32)).astype(x.dtype)

def adaln(cond, w_mod, b_mod):
    m = jnp.dot(jax.nn.silu(cond), w_mod) + b_mod
    return jnp.split(m[..., None, :], 6, axis=-1)

def modulate(h, shift, scale):
    return h * (1.0 + scale) + shift

def axial_rope_tables(n_rows):
    row = jnp.repeat(jnp.arange(n_rows), GRID_W).astype(jnp.float32)
    col = jnp.tile(jnp.arange(GRID_W), n_rows).astype(jnp.float32)
    half = ATTN_HEAD_DIM // 2
    inv_freq = ROPE_THETA ** (-jnp.arange(0, half, 2, dtype=jnp.float32) / half)
    ang = jnp.concatenate([row[:, None] * inv_freq, col[:, None] * inv_freq], axis=-1)
    return jnp.cos(ang), jnp.sin(ang)

def apply_rope(x, cos, sin):
    x1 = x[..., 0::2].astype(jnp.float32)
    x2 = x[..., 1::2].astype(jnp.float32)
    y1 = x1 * cos - x2 * sin
    y2 = x1 * sin + x2 * cos
    return jnp.stack([y1, y2], axis=-1).reshape(x.shape).astype(x.dtype)

def project_inputs(h, w_in, q_g, k_g):
    B, L, _ = h.shape
    proj = jnp.einsum('bld,de->ble', h, w_in)
    q, k, v, u_pool, a_conv, b_conv = jnp.split(proj, list(SPLITS), axis=-1)
    q = rms_norm(q.reshape(B, L, ATTN_HEADS, 2, ATTN_HEAD_DIM), q_g).transpose(0, 2, 3, 1, 4)
    k = rms_norm(k.reshape(B, L, ATTN_HEADS, 2, ATTN_HEAD_DIM), k_g).transpose(0, 2, 3, 1, 4)
    v = v.reshape(B, L, ATTN_HEADS, ATTN_V_DIM).transpose(0, 2, 1, 3)
    return q, k, v, u_pool, a_conv, b_conv

def diff_attention(q, k_all, v_all, lam):
    B, H, _, Lq, dh = q.shape
    nb = Lq // BLOCK_Q
    qb = q.reshape(B, H, 2, nb, BLOCK_Q, dh).transpose(3, 0, 1, 2, 4, 5)
    scale = dh ** -0.5

    def one_block(q_blk):
        s = jnp.einsum('bhcqd,bhckd->bhcqk', q_blk, k_all).astype(jnp.float32) * scale
        p = jax.nn.softmax(s, axis=-1)
        a = p[:, :, 0] - lam * p[:, :, 1]
        return jnp.einsum('bhqk,bhkd->bhqd', a.astype(v_all.dtype), v_all)

    o = lax.map(one_block, qb)
    return o.transpose(1, 2, 0, 3, 4).reshape(B, H, Lq, v_all.shape[-1])

def diff_attn_post(o, subln_g, lambda_init):
    B, H, L, dv = o.shape
    o = rms_norm(o, subln_g) * (1.0 - lambda_init)
    return o.transpose(0, 2, 1, 3).reshape(B, L, H * dv)

def multiscale_pool(u):
    B, L, C = u.shape
    uf = u.astype(jnp.float32)
    csum = jnp.concatenate([jnp.zeros((B, 1, C), jnp.float32), jnp.cumsum(uf, axis=1)], axis=1)
    t = jnp.arange(L)
    outs = []
    for gi, w in enumerate(POOL_WINDOWS):
        lo = jnp.clip(t - w // 2, 0, L)
        hi = jnp.clip(t + w - w // 2, 0, L)
        sl = slice(gi * POOL_GROUP, (gi + 1) * POOL_GROUP)
        seg = csum[:, :, sl]
        cnt = (hi - lo).astype(jnp.float32)[None, :, None]
        outs.append((seg[:, hi] - seg[:, lo]) / cnt - uf[:, :, sl])
    return jnp.concatenate(outs, axis=-1).astype(u.dtype)

def pool_mixer(u, pool_w, pool_scale):
    B, L, _ = u.shape
    p = multiscale_pool(u).reshape(B, L, len(POOL_WINDOWS), POOL_GROUP)
    y = jnp.einsum('blgc,gce->blge', p, pool_w).reshape(B, L, POOL_WIDTH)
    return y * pool_scale

def conformer_conv(a, b, dw_w, dw_b, ln_g, ln_b):
    u = a * jax.nn.sigmoid(b)
    y = lax.conv_general_dilated(
        u, dw_w[:, None, :].astype(u.dtype), window_strides=(1,),
        padding=((CONV_PAD, CONV_PAD),), dimension_numbers=('NWC', 'WIO', 'NWC'),
        feature_group_count=CONV_WIDTH)
    y = layer_norm(y + dw_b, ln_g, ln_b)
    return jax.nn.silu(y)

def swiglu(h, w_in, w_out):
    gu = jnp.einsum('bld,de->ble', h, w_in)
    g, u = jnp.split(gu, 2, axis=-1)
    return jnp.einsum('blf,fd->bld', jax.nn.silu(g) * u, w_out)

def first_inputs(seed: int = 0) -> dict:
    key = jax.random.key(seed)
    ks = jax.random.split(key, 26)
    f32 = jnp.float32
    n = lambda k, s: jax.random.normal(k, s, f32)
    return {
        "x": n(ks[0], (BATCH, SEQ, D_MODEL)),
        "c": n(ks[1], (BATCH, D_MODEL)),
        "ctx": n(ks[2], (BATCH, CTX_LEN, D_MODEL)),
        "c_ctx": n(ks[3], (D_MODEL,)),
        "w_mod": n(ks[4], (DEPTH, D_MODEL, 6 * D_MODEL)) * (0.5 * D_MODEL ** -0.5),
        "b_mod": n(ks[5], (DEPTH, 6 * D_MODEL)) * 0.01,
        "norm1_g": 1.0 + 0.02 * n(ks[6], (DEPTH, D_MODEL)),
        "w_in": n(ks[7], (DEPTH, D_MODEL, IN_WIDTH)) * D_MODEL ** -0.5,
        "q_norm_g": 1.0 + 0.02 * n(ks[8], (DEPTH, ATTN_HEAD_DIM)),
        "k_norm_g": 1.0 + 0.02 * n(ks[9], (DEPTH, ATTN_HEAD_DIM)),
        "lambda_q1": 0.1 * n(ks[10], (DEPTH, ATTN_HEAD_DIM)),
        "lambda_k1": 0.1 * n(ks[11], (DEPTH, ATTN_HEAD_DIM)),
        "lambda_q2": 0.1 * n(ks[12], (DEPTH, ATTN_HEAD_DIM)),
        "lambda_k2": 0.1 * n(ks[13], (DEPTH, ATTN_HEAD_DIM)),
        "subln_g": 1.0 + 0.02 * n(ks[14], (DEPTH, ATTN_V_DIM)),
        "pool_w": n(ks[15], (DEPTH, len(POOL_WINDOWS), POOL_GROUP, POOL_GROUP)) * POOL_GROUP ** -0.5,
        "pool_scale": 1.0 + 0.02 * n(ks[16], (DEPTH, POOL_WIDTH)),
        "conv_dw_w": n(ks[17], (DEPTH, CONV_KERNEL, CONV_WIDTH)) * CONV_KERNEL ** -0.5,
        "conv_dw_b": 0.01 * n(ks[18], (DEPTH, CONV_WIDTH)),
        "conv_ln_g": 1.0 + 0.02 * n(ks[19], (DEPTH, CONV_WIDTH)),
        "conv_ln_b": 0.01 * n(ks[20], (DEPTH, CONV_WIDTH)),
        "w_out": n(ks[21], (DEPTH, MIX_WIDTH, D_MODEL)) * MIX_WIDTH ** -0.5,
        "norm2_g": 1.0 + 0.02 * n(ks[22], (DEPTH, D_MODEL)),
        "w_ffn_in": n(ks[23], (DEPTH, D_MODEL, 2 * FFN_HIDDEN)) * D_MODEL ** -0.5,
        "w_ffn_out": n(ks[24], (DEPTH, FFN_HIDDEN, D_MODEL)) * FFN_HIDDEN ** -0.5,
    }

def first_block(x, c, ctx, c_ctx, w_mod, b_mod, norm1_g, w_in, q_norm_g, k_norm_g,
              lambda_q1, lambda_k1, lambda_q2, lambda_k2, subln_g, pool_w, pool_scale,
              conv_dw_w, conv_dw_b, conv_ln_g, conv_ln_b, w_out, norm2_g, w_ffn_in,
              w_ffn_out):
    B, L, _ = x.shape
    rows = L // GRID_W
    cos, sin = axial_rope_tables(rows)
    xc = ctx
    for l in range(DEPTH):
        last = l == DEPTH - 1
        lambda_init = 0.8 - 0.6 * math.exp(-0.3 * l)
        lam = (jnp.exp(jnp.sum(lambda_q1[l] * lambda_k1[l]).astype(jnp.float32))
               - jnp.exp(jnp.sum(lambda_q2[l] * lambda_k2[l]).astype(jnp.float32))
               + lambda_init)
        sh1, sc1, g1, sh2, sc2, g2 = adaln(c, w_mod[l], b_mod[l])
        csh1, csc1, cg1, csh2, csc2, cg2 = adaln(c_ctx, w_mod[l], b_mod[l])

        h = modulate(rms_norm(x, norm1_g[l]), sh1, sc1)
        hc = modulate(rms_norm(xc, norm1_g[l]), csh1, csc1)
        q, k, v, up, ca, cb = project_inputs(h, w_in[l], q_norm_g[l], k_norm_g[l])
        qc, kc, vc, upc, cac, cbc = project_inputs(hc, w_in[l], q_norm_g[l], k_norm_g[l])
        q = apply_rope(q, cos, sin)
        k = apply_rope(k, cos, sin)
        k_all = jnp.concatenate([kc, k], axis=3)
        v_all = jnp.concatenate([vc, v], axis=2)
        attn = diff_attn_post(diff_attention(q, k_all, v_all, lam), subln_g[l], lambda_init)
        pool_o = pool_mixer(up, pool_w[l], pool_scale[l])
        conv_o = conformer_conv(ca, cb, conv_dw_w[l], conv_dw_b[l], conv_ln_g[l], conv_ln_b[l])
        mix = jnp.concatenate([attn, pool_o, conv_o], axis=-1)
        x = x + g1 * jnp.einsum('blm,md->bld', mix, w_out[l])

        x = x + g2 * swiglu(modulate(rms_norm(x, norm2_g[l]), sh2, sc2), w_ffn_in[l], w_ffn_out[l])

        if not last:
            attn_c = diff_attn_post(diff_attention(qc, kc, vc, lam), subln_g[l], lambda_init)
            pool_c = pool_mixer(upc, pool_w[l], pool_scale[l])
            conv_c = conformer_conv(cac, cbc, conv_dw_w[l], conv_dw_b[l], conv_ln_g[l], conv_ln_b[l])
            mix_c = jnp.concatenate([attn_c, pool_c, conv_c], axis=-1)
            xc = xc + cg1 * jnp.einsum('blm,md->bld', mix_c, w_out[l])
            xc = xc + cg2 * swiglu(modulate(rms_norm(xc, norm2_g[l]), csh2, csc2),
                                   w_ffn_in[l], w_ffn_out[l])
    return x


DEPTH_2 = 1

HEAD_DIM = 64
BRANCH_WIDTH = D_MODEL // 2
N_BRANCHES = 4
Q_BLOCK = 128
FOX_HEADS = BRANCH_WIDTH // HEAD_DIM
LRU_BLOCKS = 8
LRU_BLOCK_DIM = BRANCH_WIDTH // LRU_BLOCKS
CONV_WIDTH_2 = 4
LRU_C = 8.0
NSA_HEADS = BRANCH_WIDTH // HEAD_DIM
NSA_KV_HEADS = 2
NSA_GROUP = NSA_HEADS // NSA_KV_HEADS
NSA_KV_WIDTH = NSA_KV_HEADS * HEAD_DIM
CMP_BLOCK = 32
CMP_STRIDE = 16
CMP_HIDDEN = 2 * HEAD_DIM
SLC_BLOCK = 64
SLC_TOPK = 16
SLC_LOCAL = 2
SLC_FORCE_SCORE = 1e6
WINDOW = 512
SG_CHUNK = 128
SG_GROUPS = 8
SG_GROUP_DIM = BRANCH_WIDTH // SG_GROUPS

NORM_EPS = 1e-6
NEG_INF = -1e30


def _in_split_sizes():
    W = BRANCH_WIDTH
    return (W, W, W, FOX_HEADS, W,
            W, W,
            W, NSA_KV_WIDTH, NSA_KV_WIDTH, NSA_KV_WIDTH,
            NSA_KV_WIDTH, NSA_KV_WIDTH, NSA_KV_WIDTH,
            3 * NSA_HEADS, W,
            W, W, W,
            N_BRANCHES * D_MODEL)

def rms_norm_2(x, g):
    x32 = x.astype(jnp.float32)
    y = x32 * lax.rsqrt(jnp.mean(x32 * x32, axis=-1, keepdims=True) + NORM_EPS)
    return (y * g.astype(jnp.float32)).astype(x.dtype)

def layer_norm_2(x, g):
    x32 = x.astype(jnp.float32)
    mu = jnp.mean(x32, axis=-1, keepdims=True)
    xc = x32 - mu
    y = xc * lax.rsqrt(jnp.mean(xc * xc, axis=-1, keepdims=True) + NORM_EPS)
    return (y * g.astype(jnp.float32)).astype(x.dtype)

def masked_softmax(s, mask):
    p = jax.nn.softmax(jnp.where(mask, s, NEG_INF), axis=-1)
    return jnp.where(mask, p, 0.0)

def fox_attention(q, k, v, f_logit):
    B, S, H, dh = q.shape
    n_blk = S // Q_BLOCK
    scale = 1.0 / math.sqrt(dh)
    c = jnp.cumsum(jax.nn.log_sigmoid(f_logit.astype(jnp.float32)), axis=1)
    c_k = c.transpose(0, 2, 1)[:, :, None, :]
    qb = q.reshape(B, n_blk, Q_BLOCK, H, dh).transpose(1, 0, 2, 3, 4)
    cb = c.reshape(B, n_blk, Q_BLOCK, H).transpose(1, 0, 2, 3)
    pos_k = jnp.arange(S)

    def block(args):
        q_i, c_i, i = args
        t = i * Q_BLOCK + jnp.arange(Q_BLOCK)
        s = jnp.einsum('bqhd,bkhd->bhqk', q_i, k).astype(jnp.float32) * scale
        s = s + c_i.transpose(0, 2, 1)[..., None] - c_k
        p = masked_softmax(s, pos_k[None, :] <= t[:, None])
        return jnp.einsum('bhqk,bkhd->bqhd', p.astype(v.dtype), v)

    out = lax.map(block, (qb, cb, jnp.arange(n_blk)))
    return out.transpose(1, 0, 2, 3, 4).reshape(B, S, H, dh)

def rg_lru(xb, conv_w, conv_b, w_a, b_a, w_x, b_x, lam):
    B, S, W = xb.shape
    xc = lax.conv_general_dilated(
        xb, conv_w.reshape(CONV_WIDTH_2, 1, W).astype(xb.dtype), window_strides=(1,),
        padding=[(CONV_WIDTH_2 - 1, 0)], dimension_numbers=('NWC', 'WIO', 'NWC'),
        feature_group_count=W) + conv_b
    xh = xc.reshape(B, S, LRU_BLOCKS, LRU_BLOCK_DIM)
    r = jax.nn.sigmoid((jnp.einsum('bsnd,nde->bsne', xh, w_a).reshape(B, S, W) + b_a).astype(jnp.float32))
    i_g = jax.nn.sigmoid((jnp.einsum('bsnd,nde->bsne', xh, w_x).reshape(B, S, W) + b_x).astype(jnp.float32))
    log_a = -LRU_C * r * jax.nn.softplus(-lam.astype(jnp.float32))
    a = jnp.exp(log_a)
    b = jnp.sqrt(-jnp.expm1(2.0 * log_a)) * (i_g * xc.astype(jnp.float32))

    def combine(left, right):
        a_l, b_l = left
        a_r, b_r = right
        return a_l * a_r, a_r * b_l + b_r

    _, h = lax.associative_scan(combine, (a, b), axis=1)
    return h.astype(xb.dtype)

def _cmp_slc_overlap(n_cmp, n_slc):
    c0 = np.arange(n_cmp) * CMP_STRIDE
    s0 = np.arange(n_slc) * SLC_BLOCK
    ov = np.minimum(c0[:, None] + CMP_BLOCK, s0[None, :] + SLC_BLOCK) - np.maximum(c0[:, None], s0[None, :])
    return (np.clip(ov, 0, None) / CMP_BLOCK).astype(np.float32)

def nsa_attention(q, k_cmp, v_cmp, k_slc, v_slc, k_win, v_win, gates,
                  kn_g, cmp_pos, wk1, wk2, wv1, wv2):
    B, S, H, dh = q.shape
    G, R = NSA_KV_HEADS, NSA_GROUP
    scale = 1.0 / math.sqrt(dh)
    n_cmp = (S - CMP_BLOCK) // CMP_STRIDE + 1
    blk_idx = np.arange(n_cmp)[:, None] * CMP_STRIDE + np.arange(CMP_BLOCK)[None, :]
    cmp_end = jnp.asarray(blk_idx[:, -1])

    def compress(t, w1, w2):
        tb = t[:, blk_idx] + cmp_pos[None, None, :, None, :]
        tb = tb.transpose(0, 1, 3, 2, 4).reshape(B, n_cmp, G, CMP_BLOCK * dh)
        return jax.nn.silu(tb @ w1) @ w2

    k_c = rms_norm_2(compress(k_cmp, wk1, wk2), kn_g)
    v_c = compress(v_cmp, wv1, wv2)
    n_slc = S // SLC_BLOCK
    top_k = min(SLC_TOPK, n_slc)
    overlap = jnp.asarray(_cmp_slc_overlap(n_cmp, n_slc))
    ks_blk = rms_norm_2(k_slc, kn_g).reshape(B, n_slc, SLC_BLOCK, G, dh).transpose(0, 3, 1, 2, 4)
    vs_blk = v_slc.reshape(B, n_slc, SLC_BLOCK, G, dh).transpose(0, 3, 1, 2, 4)
    kw_pad = jnp.pad(rms_norm_2(k_win, kn_g), ((0, 0), (WINDOW, 0), (0, 0), (0, 0)))
    vw_pad = jnp.pad(v_win, ((0, 0), (WINDOW, 0), (0, 0), (0, 0)))
    span = WINDOW + Q_BLOCK

    n_blk = S // Q_BLOCK
    qg = q.reshape(B, n_blk, Q_BLOCK, G, R, dh).transpose(1, 0, 2, 3, 4, 5)
    gb = gates.reshape(B, n_blk, Q_BLOCK, 3, H).transpose(1, 0, 2, 3, 4)
    b_ix = jnp.arange(B)[:, None, None, None]
    g_ix = jnp.arange(G)[None, :, None, None]
    j = jnp.arange(n_slc)

    def block(args):
        q_i, g_i, i = args
        t = i * Q_BLOCK + jnp.arange(Q_BLOCK)
        s_c = jnp.einsum('bqgrd,bcgd->bgrqc', q_i, k_c).astype(jnp.float32) * scale
        p_c = masked_softmax(s_c, cmp_end[None, :] <= t[:, None])
        o_c = jnp.einsum('bgrqc,bcgd->bqgrd', p_c.astype(v_c.dtype), v_c)
        imp = jnp.einsum('bgrqc,cj->bgqj', p_c, overlap)
        jt = t // SLC_BLOCK
        valid = j[None, :] <= jt[:, None]
        forced = (j[None, :] == 0) | (valid & (j[None, :] > jt[:, None] - SLC_LOCAL))
        score = jnp.where(forced, SLC_FORCE_SCORE, jnp.where(valid, imp, -1.0))
        top_val, top_idx = lax.top_k(score, top_k)
        k_sel = ks_blk[b_ix, g_ix, top_idx]
        v_sel = vs_blk[b_ix, g_ix, top_idx]
        key_pos = top_idx[..., None] * SLC_BLOCK + jnp.arange(SLC_BLOCK)
        m_s = (top_val >= 0.0)[..., None] & (key_pos <= t[None, None, :, None, None])
        s_s = jnp.einsum('bqgrd,bgqkld->bgrqkl', q_i, k_sel).astype(jnp.float32) * scale
        n_sel = top_k * SLC_BLOCK
        p_s = masked_softmax(s_s.reshape(B, G, R, Q_BLOCK, n_sel), m_s.reshape(B, G, 1, Q_BLOCK, n_sel))
        o_s = jnp.einsum('bgrqn,bgqnd->bqgrd', p_s.astype(v_sel.dtype),
                         v_sel.reshape(B, G, Q_BLOCK, n_sel, dh))
        k_wi = lax.dynamic_slice_in_dim(kw_pad, i * Q_BLOCK, span, axis=1)
        v_wi = lax.dynamic_slice_in_dim(vw_pad, i * Q_BLOCK, span, axis=1)
        pos_w = i * Q_BLOCK - WINDOW + jnp.arange(span)
        m_w = (pos_w[None, :] >= 0) & (pos_w[None, :] <= t[:, None]) & (pos_w[None, :] > t[:, None] - WINDOW)
        s_w = jnp.einsum('bqgrd,bkgd->bgrqk', q_i, k_wi).astype(jnp.float32) * scale
        p_w = masked_softmax(s_w, m_w)
        o_w = jnp.einsum('bgrqk,bkgd->bqgrd', p_w.astype(v_wi.dtype), v_wi)
        g = g_i.reshape(B, Q_BLOCK, 3, G, R)[..., None]
        return g[:, :, 0] * o_c + g[:, :, 1] * o_s + g[:, :, 2] * o_w

    out = lax.map(block, (qg, gb, jnp.arange(n_blk)))
    return out.transpose(1, 0, 2, 3, 4, 5).reshape(B, S, H * dh)

def spatial_gating(u, v, ln_g, w_s, b_s):
    B, S, W = u.shape
    n_chunk = S // SG_CHUNK
    u = jax.nn.gelu(u, approximate=False)
    v = layer_norm_2(jax.nn.gelu(v, approximate=False), ln_g)
    vc = v.reshape(B, n_chunk, SG_CHUNK, SG_GROUPS, SG_GROUP_DIM)
    causal = jnp.tril(jnp.ones((SG_CHUNK, SG_CHUNK), dtype=w_s.dtype))
    mixed = jnp.einsum('gts,bcsgd->bctgd', w_s * causal, vc) + b_s.T[None, None, :, :, None]
    return u * mixed.reshape(B, S, W)

def hybrid_layer(x, norm_g, w_in, b_forget, qn_a, kn_a, conv_w, conv_b, w_rg_a, b_rg_a,
                 w_rg_x, b_rg_x, lru_lambda, qn_c, kn_c, cmp_pos, cmp_k_w1, cmp_k_w2,
                 cmp_v_w1, cmp_v_w2, ln_v_g, w_spatial, b_spatial, w_branch, w_out):
    B, S, D = x.shape
    W = BRANCH_WIDTH
    xn = rms_norm_2(x, norm_g)
    z = xn @ w_in
    split_at = np.cumsum(_in_split_sizes())[:-1].tolist()
    (qa, ka, va, fa, ga, xb, gb, qc, kcc, vcc, ksc, vsc, kwc, vwc, gate_c, gc,
     ud, vd, gd, mg) = jnp.split(z, split_at, axis=-1)
    heads = lambda t, n: t.reshape(B, S, n, HEAD_DIM)
    y_a = fox_attention(rms_norm_2(heads(qa, FOX_HEADS), qn_a), rms_norm_2(heads(ka, FOX_HEADS), kn_a),
                        heads(va, FOX_HEADS), fa + b_forget).reshape(B, S, W)
    y_b = rg_lru(xb, conv_w, conv_b, w_rg_a, b_rg_a, w_rg_x, b_rg_x, lru_lambda)
    y_c = nsa_attention(rms_norm_2(heads(qc, NSA_HEADS), qn_c),
                        heads(kcc, NSA_KV_HEADS), heads(vcc, NSA_KV_HEADS),
                        heads(ksc, NSA_KV_HEADS), heads(vsc, NSA_KV_HEADS),
                        heads(kwc, NSA_KV_HEADS), heads(vwc, NSA_KV_HEADS),
                        jax.nn.sigmoid(gate_c).reshape(B, S, 3, NSA_HEADS),
                        kn_c, cmp_pos, cmp_k_w1, cmp_k_w2, cmp_v_w1, cmp_v_w2)
    y_d = spatial_gating(ud, vd, ln_v_g, w_spatial, b_spatial)
    ys = jnp.stack([y_a * jax.nn.silu(ga), y_b * jax.nn.silu(gb),
                    y_c * jax.nn.silu(gc), y_d * jax.nn.silu(gd)], axis=2)
    proj = jnp.einsum('bsnw,nwd->bsnd', ys, w_branch)
    merged = jnp.sum(jax.nn.sigmoid(mg.reshape(B, S, N_BRANCHES, D)) * proj, axis=2)
    return x + merged @ w_out

def second_inputs(seed: int = 0) -> dict:
    key = jax.random.key(seed)
    ks = iter(jax.random.split(key, 32))
    L, D, W, dh = DEPTH_2, D_MODEL, BRANCH_WIDTH, HEAD_DIM

    def nrm(shape, scale):
        return jax.random.normal(next(ks), shape, jnp.float32) * scale

    w_in_width = sum(_in_split_sizes())
    x = nrm((BATCH, SEQ, D), 1.0)
    norm_g = 1.0 + nrm((L, D), 0.05)
    w_in = nrm((L, D, w_in_width), D ** -0.5)
    b_forget = 3.0 + nrm((L, FOX_HEADS), 0.5)
    qn_a = 1.0 + nrm((L, dh), 0.05)
    kn_a = 1.0 + nrm((L, dh), 0.05)
    conv_w = nrm((L, CONV_WIDTH_2, W), CONV_WIDTH_2 ** -0.5)
    conv_b = nrm((L, W), 0.01)
    w_rg_a = nrm((L, LRU_BLOCKS, LRU_BLOCK_DIM, LRU_BLOCK_DIM), LRU_BLOCK_DIM ** -0.5)
    b_rg_a = nrm((L, W), 0.01)
    w_rg_x = nrm((L, LRU_BLOCKS, LRU_BLOCK_DIM, LRU_BLOCK_DIM), LRU_BLOCK_DIM ** -0.5)
    b_rg_x = nrm((L, W), 0.01)
    a_c = jax.random.uniform(next(ks), (L, W), jnp.float32, 0.9, 0.999)
    a0 = a_c ** (1.0 / LRU_C)
    lru_lambda = jnp.log(a0) - jnp.log1p(-a0)
    qn_c = 1.0 + nrm((L, dh), 0.05)
    kn_c = 1.0 + nrm((L, dh), 0.05)
    cmp_pos = nrm((L, CMP_BLOCK, dh), 0.02)
    cmp_k_w1 = nrm((L, CMP_BLOCK * dh, CMP_HIDDEN), (CMP_BLOCK * dh) ** -0.5)
    cmp_k_w2 = nrm((L, CMP_HIDDEN, dh), CMP_HIDDEN ** -0.5)
    cmp_v_w1 = nrm((L, CMP_BLOCK * dh, CMP_HIDDEN), (CMP_BLOCK * dh) ** -0.5)
    cmp_v_w2 = nrm((L, CMP_HIDDEN, dh), CMP_HIDDEN ** -0.5)
    ln_v_g = 1.0 + nrm((L, W), 0.05)
    w_spatial = nrm((L, SG_GROUPS, SG_CHUNK, SG_CHUNK), SG_CHUNK ** -0.5)
    b_spatial = 1.0 + nrm((L, SG_GROUPS, SG_CHUNK), 0.1)
    w_branch = nrm((L, N_BRANCHES, W, D), W ** -0.5)
    w_out = nrm((L, D, D), D ** -0.5)
    return {"x": x, "norm_g": norm_g, "w_in": w_in, "b_forget": b_forget, "qn_a": qn_a,
            "kn_a": kn_a, "conv_w": conv_w, "conv_b": conv_b, "w_rg_a": w_rg_a,
            "b_rg_a": b_rg_a, "w_rg_x": w_rg_x, "b_rg_x": b_rg_x, "lru_lambda": lru_lambda,
            "qn_c": qn_c, "kn_c": kn_c, "cmp_pos": cmp_pos, "cmp_k_w1": cmp_k_w1,
            "cmp_k_w2": cmp_k_w2, "cmp_v_w1": cmp_v_w1, "cmp_v_w2": cmp_v_w2,
            "ln_v_g": ln_v_g, "w_spatial": w_spatial, "b_spatial": b_spatial,
            "w_branch": w_branch, "w_out": w_out}

def second_block(x, norm_g, w_in, b_forget, qn_a, kn_a, conv_w, conv_b, w_rg_a, b_rg_a,
              w_rg_x, b_rg_x, lru_lambda, qn_c, kn_c, cmp_pos, cmp_k_w1, cmp_k_w2,
              cmp_v_w1, cmp_v_w2, ln_v_g, w_spatial, b_spatial, w_branch, w_out):
    for l in range(DEPTH_2):
        x = hybrid_layer(x, norm_g[l], w_in[l], b_forget[l], qn_a[l], kn_a[l], conv_w[l],
                         conv_b[l], w_rg_a[l], b_rg_a[l], w_rg_x[l], b_rg_x[l], lru_lambda[l],
                         qn_c[l], kn_c[l], cmp_pos[l], cmp_k_w1[l], cmp_k_w2[l], cmp_v_w1[l],
                         cmp_v_w2[l], ln_v_g[l], w_spatial[l], b_spatial[l], w_branch[l], w_out[l])
    return x


def setup_inputs(seed=0):
    out = dict(first_inputs(seed))
    for name, value in second_inputs(seed + 1).items():
        if name != "x":
            out[name + "_2"] = value
    return out


def reference(
    x, c, ctx, c_ctx, w_mod, b_mod, norm1_g, w_in, q_norm_g, k_norm_g, lambda_q1, lambda_k1,
    lambda_q2, lambda_k2, subln_g, pool_w, pool_scale, conv_dw_w, conv_dw_b, conv_ln_g,
    conv_ln_b, w_out, norm2_g, w_ffn_in, w_ffn_out, norm_g_2, w_in_2, b_forget_2, qn_a_2,
    kn_a_2, conv_w_2, conv_b_2, w_rg_a_2, b_rg_a_2, w_rg_x_2, b_rg_x_2, lru_lambda_2, qn_c_2,
    kn_c_2, cmp_pos_2, cmp_k_w1_2, cmp_k_w2_2, cmp_v_w1_2, cmp_v_w2_2, ln_v_g_2, w_spatial_2,
    b_spatial_2, w_branch_2, w_out_2,
):
    x = first_block(
        x, c, ctx, c_ctx, w_mod, b_mod, norm1_g, w_in, q_norm_g, k_norm_g, lambda_q1, lambda_k1,
        lambda_q2, lambda_k2, subln_g, pool_w, pool_scale, conv_dw_w, conv_dw_b, conv_ln_g,
        conv_ln_b, w_out, norm2_g, w_ffn_in, w_ffn_out,
    )
    return second_block(
        x, norm_g_2, w_in_2, b_forget_2, qn_a_2, kn_a_2, conv_w_2, conv_b_2, w_rg_a_2, b_rg_a_2,
        w_rg_x_2, b_rg_x_2, lru_lambda_2, qn_c_2, kn_c_2, cmp_pos_2, cmp_k_w1_2, cmp_k_w2_2,
        cmp_v_w1_2, cmp_v_w2_2, ln_v_g_2, w_spatial_2, b_spatial_2, w_branch_2, w_out_2,
    )


_drawn_inputs = setup_inputs


def setup_inputs(seed=0):
    import zlib

    import numpy as np

    out = dict(_drawn_inputs(seed))
    spreads = {}
    factors = {'norm1_g': 7.964,
     'q_norm_g': 8.0,
     'k_norm_g': 8.0,
     'lambda_q1': 5.216,
     'lambda_k1': 8.0,
     'subln_g': 64.0,
     'pool_scale': 8.0,
     'conv_dw_b': 64.0,
     'conv_ln_g': 64.0,
     'conv_ln_b': 64.0,
     'norm2_g': 6.312,
     'b_forget_2': 24.464,
     'qn_a_2': 200.0,
     'kn_a_2': 200.0,
     'conv_b_2': 200.0,
     'b_rg_a_2': 200.0,
     'b_rg_x_2': 200.0,
     'qn_c_2': 64.0,
     'kn_c_2': 64.0,
     'cmp_pos_2': 64.0,
     'ln_v_g_2': 64.0,
     'b_spatial_2': 25.584,
     'lambda_q2': 8.0,
     'lambda_k2': 8.0,
     'norm_g_2': 5.6,
     'conv_w_2': 54.784,
     'w_rg_a_2': 64.0,
     'w_rg_x_2': 64.0,
     'lru_lambda_2': 64.0,
     'cmp_k_w1_2': 8.0,
     'cmp_k_w2_2': 8.0,
     'cmp_v_w1_2': 8.0,
     'cmp_v_w2_2': 8.0}
    for name, (base, spread) in spreads.items():
        noise = np.random.default_rng([zlib.crc32(name.encode()), seed]).standard_normal(out[name].shape)
        drawn = base * np.exp(spread * noise) if base else spread * noise
        out[name] = __import__('jax').numpy.asarray(drawn.astype(out[name].dtype))
    for name, factor in factors.items():
        out[name] = (out[name] * factor).astype(out[name].dtype)
    return out
```

```python
import math
from contextlib import ExitStack

import numpy as np

import concourse.bass as bass
from concourse import mybir

ACT = mybir.ActivationFunctionType
ALU = mybir.AluOpType
AX = mybir.AxisListType
F32 = mybir.dt.float32
F32R = mybir.dt.float32r

P = 128
D = 1024
KC = D // P
S = 256
T = 2 * S
DEPTH = 2
HEADS = 4
DH = 64
FFN = 2816
FC = FFN // P
TAPS = 31
PAD = TAPS // 2
EPS = 1e-6
THETA = 10000.0
GRID_W = 64
WINDOWS = (2, 4, 8, 16)
UPAD = 8
LRU_C = 8.0
NH2 = 8
CMP_BLOCK, CMP_STRIDE = 32, 16
NCMP = (S - CMP_BLOCK) // CMP_STRIDE + 1
MASKED = -1e30

BLK = 8
SLOT = BLK * P
RAW = 4
SPLIT = 4

QK = 512
IN_Q, IN_K, IN_V, IN_UP, IN_A, IN_B = 0, 512, 1024, 1536, 1792, 2048
W2 = 512
Z = {}
_at = 0
for _n, _w in (("qa", W2), ("ka", W2), ("va", W2), ("fa", 8), ("ga", W2), ("xb", W2), ("gb", W2), ("qc", W2),
               ("kcc", 128), ("vcc", 128), ("ksc", 128), ("vsc", 128), ("kwc", 128), ("vwc", 128), ("gate", 24),
               ("gc", W2), ("ud", W2), ("vd", W2), ("gd", W2), ("mg", 4 * D)):
    Z[_n] = (_at, _w)
    _at += _w
Z_WIDTH = _at
GATE_ROW = 32


def stream_order():
    def layer(l):
        a = [(f"q{c}", 8) for c in range(4)] + [(f"k{c}", 8) for c in range(4)] + [("v", 32)]
        a += [(n, 8) for n in ("up0", "up1", "cb0", "ca0", "cb1", "ca1")]
        b = [(f"wo{d}", 8) for d in range(8)]
        for j in range(FC):
            b += [(f"g{j}", 8), (f"u{j}", 8)]
        b += [(f"fo{d}", FC) for d in range(8)]
        return [(f"{n}.{l}", k) for n, k in a], [(f"{n}.{l}", k) for n, k in b]

    def mod(l, lo, hi):
        return [(f"mod{g}.{l}", 32) for g in range(lo, hi)]

    a0, b0 = layer(0)
    a1, b1 = layer(1)
    second = [(f"{n}{c}", 8) for n in ("qa", "ka", "qc") for c in range(4)] + [("ks0", 8), ("kw0", 8)]
    second += [("va", 32), ("vsw", 16), ("fg", 8), ("kcc", 8), ("vcc", 8)]
    second += [(f"xb{c}", 8) for c in range(4)] + [(f"ud{c}", 8) for c in range(4)] + [("vd", 32)]
    second += [(f"G{c}", 8) for c in range(16)] + [(f"mg{c}", 8) for c in range(32)]
    second += [(f"br{d}_{n}", 4) for d in range(8) for n in range(4)] + [(f"wo{d}.2", 8) for d in range(8)]
    return mod(0, 0, 4) + a0 + mod(0, 4, 12) + mod(1, 0, 4) + b0 + a1 + mod(1, 4, 12) + b1 + second


def weight_stream(w_mod, w_in, w_out, w_ffn_in, w_ffn_out, w_in_2, w_branch_2, w_out_2):
    def cols(w, c, k=KC):
        return np.ascontiguousarray(w[:, c:c + P]).reshape(k, P, P)

    def wide(w, c, n):
        return w[:, c:c + n].reshape(KC, P, n // P, P).transpose(0, 2, 1, 3).reshape(-1, P, P)

    z = {n: w_in_2[0][:, a:a + w] for n, (a, w) in Z.items()}
    z["qc"] = z["qc"].reshape(D, 2, 4, DH).transpose(0, 2, 1, 3).reshape(D, W2)
    fg = np.zeros((D, P), np.float32)
    fg[:, 0:8] = z["fa"]
    fg[:, GATE_ROW:GATE_ROW + 24] = z["gate"]
    vsw = np.concatenate([z["vsc"], z["vwc"]], axis=1)
    gates = np.concatenate([z["ga"], z["gb"], z["gc"], z["gd"]], axis=1)
    parts = []
    for name, blocks in stream_order():
        n, _, l = name.partition(".")
        if n.startswith("mod"):
            parts.append(wide(w_mod[int(l)], int(n[3:]) * 512, 512))
        elif n.startswith("br"):
            d, b = n[2:].split("_")
            parts.append(cols(w_branch_2[0][int(b)], int(d) * P, 4))
        elif l == "2":
            parts.append(cols(w_out_2[0], int(n[2:]) * P))
        elif l:
            l = int(l)
            if n == "v":
                parts.append(wide(w_in[l], IN_V, 512))
            elif n[:2] in ("up", "ca", "cb"):
                parts.append(cols(w_in[l], {"up": IN_UP, "ca": IN_A, "cb": IN_B}[n[:2]] + int(n[2:]) * P))
            elif n[:2] == "wo":
                parts.append(cols(w_out[l], int(n[2:]) * P))
            elif n[:2] == "fo":
                parts.append(cols(w_ffn_out[l], int(n[2:]) * P, FC))
            elif n[0] in "gu":
                parts.append(cols(w_ffn_in[l], (n[0] == "u") * FFN + int(n[1:]) * P))
            else:
                parts.append(cols(w_in[l], {"q": IN_Q, "k": IN_K}[n[0]] + int(n[1:]) * P))
        elif n in ("va", "vd"):
            parts.append(wide(z[n], 0, W2))
        elif n == "vsw":
            parts.append(wide(vsw, 0, 256))
        elif n == "fg":
            parts.append(cols(fg, 0))
        elif n in ("kcc", "vcc"):
            parts.append(cols(z[n], 0))
        elif n in ("ks0", "kw0"):
            parts.append(cols(z[n[:2] + "c"], 0))
        elif n[0] == "G":
            parts.append(cols(gates, int(n[1:]) * P))
        else:
            parts.append(cols(z[n[:2]], int(n[2:]) * P))
        assert len(parts[-1]) == blocks, name
    flat = np.concatenate(parts)
    return np.ascontiguousarray(flat.reshape(-1, BLK, P, P).transpose(0, 2, 1, 3)).reshape(-1, P, SLOT)


def columns():
    at, out = 0, {}
    for n, w in (("c", 2 * KC), ("n1", 16), ("n2", 16), ("bmod", 96), ("qg", 2), ("kg", 2), ("la", 4), ("lb", 4),
                 ("sub", 2), ("ps", 4), ("cw", 4 * TAPS), ("cb", 4), ("lg", 4), ("lb2", 4),
                 ("ng2", 8), ("bf", 1), ("qna", 1), ("kna", 1), ("qnc", 1), ("knc", 1), ("w4", 16), ("b4", 4),
                 ("bra", 4), ("brx", 4), ("lam", 4), ("lnv", 4), ("pos", CMP_BLOCK)):
        out[n] = (at, w)
        at += w
    return out, at


def const_columns():
    at, out = 0, {}
    for n, w in (("ident", P), ("ones", P), ("blk", P), ("rot", P), ("cos", S), ("sin", S), ("icnt", 2 * S), ("pair", 2)):
        out[n] = (at, w)
        at += w
    first = at
    for n, w in (("cmask", 384), ("tril", P), ("cmpm", 2 * 16), ("cmp01", 2 * 16), ("ones2", S)):
        out[n] = (at, w)
        at += w
    return out, at, first


def shape_constants():
    cc, width, _ = const_columns()
    c = np.zeros((P, width), np.float32)

    def put(n, v):
        c[:, cc[n][0]:cc[n][0] + cc[n][1]] = v.reshape(P, -1)

    p = np.arange(P)
    put("ident", np.eye(P))
    put("ones", np.ones((P, P)))
    put("blk", (p[:, None] // DH == p[None, :] // DH))
    rot = np.zeros((P, P))
    rot[p[1::2], p[0::2]] = -1
    rot[p[0::2], p[1::2]] = 1
    put("rot", rot)
    t = np.arange(S)
    half = DH // 2
    inv = (np.float32(THETA) ** (-np.arange(0, half, 2, dtype=np.float32) / np.float32(half))).astype(np.float32)
    ang = np.concatenate([(t // GRID_W).astype(np.float32)[:, None] * inv, (t % GRID_W).astype(np.float32)[:, None] * inv], axis=-1)
    ang = ang[:, (p % DH) // 2].T.astype(np.float64)
    put("cos", np.cos(ang))
    put("sin", np.sin(ang))
    icnt = np.zeros((P, 2, S))
    for g, w in enumerate(WINDOWS):
        n = np.clip(t + w - w // 2, 0, S) - np.clip(t - w // 2, 0, S)
        icnt[g % 2 * DH:g % 2 * DH + DH, g // 2] = 1.0 / n
    put("icnt", icnt)
    put("pair", (p[:, None] % 2 == np.arange(2)[None, :]) & (p[:, None] < 4))
    causal = np.where(p[None, :] <= p[:, None], 0.0, MASKED)
    put("cmask", np.concatenate([causal, np.zeros((P, P)), causal], axis=1))
    put("tril", (p[None, :] >= p[:, None]))
    ends = np.arange(16) * CMP_STRIDE + CMP_BLOCK - 1
    ok = np.stack([(ends[None, :] <= (p + q * P)[:, None]) & (np.arange(16) < NCMP)[None, :] for q in range(2)], axis=1)
    put("cmpm", np.where(ok, 0.0, MASKED))
    put("cmp01", ok)
    put("ones2", np.ones((P, S)))
    return c


def parameter_columns(i):
    pc, width = columns()
    c = np.zeros((P, width), np.float32)

    def put(n, v, rows=P):
        a, w = pc[n]
        c[:rows, a:a + w] = v

    def feat(v, k):
        return np.asarray(v).reshape(-1, k, P).transpose(2, 0, 1).reshape(P, -1)

    put("c", np.stack([i["c_ctx"].reshape(KC, P), i["c"].reshape(KC, P)], axis=-1).transpose(1, 0, 2).reshape(P, -1))
    put("n1", feat(i["norm1_g"], KC))
    put("n2", feat(i["norm2_g"], KC))
    put("bmod", feat(i["b_mod"], 48))
    put("qg", np.tile(i["q_norm_g"], 2).T)
    put("kg", np.tile(i["k_norm_g"], 2).T)
    put("la", np.stack([i["lambda_q1"], i["lambda_q2"]], 1).reshape(4, DH).T, DH)
    put("lb", np.stack([i["lambda_k1"], i["lambda_k2"]], 1).reshape(4, DH).T, DH)
    put("sub", i["subln_g"].T)
    put("ps", feat(i["pool_scale"], 2))
    put("cw", i["conv_dw_w"].reshape(DEPTH, TAPS, 2, P).transpose(3, 0, 2, 1).reshape(P, -1))
    put("cb", feat(i["conv_dw_b"], 2))
    put("lg", feat(i["conv_ln_g"], 2))
    put("lb2", feat(i["conv_ln_b"], 2))
    put("ng2", feat(i["norm_g_2"], KC))
    put("bf", i["b_forget_2"].reshape(8, 1), 8)
    for n, k in (("qna", "qn_a_2"), ("kna", "kn_a_2"), ("qnc", "qn_c_2"), ("knc", "kn_c_2")):
        put(n, np.tile(i[k], 2).T)
    put("w4", i["conv_w_2"].reshape(4, 4, P).transpose(2, 1, 0).reshape(P, -1))
    put("b4", feat(i["conv_b_2"], 4))
    put("bra", feat(i["b_rg_a_2"], 4))
    put("brx", feat(i["b_rg_x_2"], 4))
    put("lam", feat(i["lru_lambda_2"], 4))
    put("lnv", feat(i["ln_v_g_2"], 4))
    put("pos", np.tile(i["cmp_pos_2"][0].T, (2, 1)))
    return c


def block_diagonal(w):
    n = len(w) // 2
    out = np.zeros((P, n, P), np.float32)
    for g in range(2 * n):
        a = g % 2 * DH
        out[a:a + DH, g // 2, a:a + DH] = w[g]
    return out


EXTRA = {"rg_ws": (0, 2048), "bs": (2048, 512), "w1k": (2560, 4096), "w1v": (6656, 4096), "w2": (10752, 128)}


def extra_weights(i):
    def w1(w):
        return np.tile(w.reshape(CMP_BLOCK, DH, P).transpose(1, 0, 2).reshape(DH, -1), (2, 1))
    bs = np.repeat(i["b_spatial_2"][0].reshape(4, 2, P).transpose(1, 0, 2), DH, axis=0)
    return np.concatenate([
        block_diagonal(i["w_rg_a_2"][0]).reshape(P, -1), block_diagonal(i["w_rg_x_2"][0]).reshape(P, -1),
        i["w_spatial_2"][0].transpose(2, 0, 1).reshape(P, -1), bs.reshape(P, -1),
        w1(i["cmp_k_w1_2"][0]), w1(i["cmp_v_w1_2"][0]), i["cmp_k_w2_2"][0], i["cmp_v_w2_2"][0]], axis=1)


class Counts:

    def __init__(self, nc, ctx, known):
        self.nc, self.ctx, self.known = nc, ctx, known
        self.sems, self.n, self.found = {}, {}, {}

    def sem(self, name):
        if name not in self.sems:
            self.sems[name] = self.ctx.enter_context(self.nc.semaphore(name))
        return self.sems[name]

    def tick(self, name, *products, by=1):
        self.n[name] = self.n.get(name, 0) + by
        for p in products:
            assert p not in self.found, p
            self.found[p] = (name, self.n[name])
        return self.sem(name), by

    def at(self, product):
        name, n = self.known.get(product, self.found.get(product, ("unknown", 1)))
        assert not self.known or product in self.known, product
        return self.sem(name), n


def program(nc, io, known):
    pc, _ = columns()
    cc, NCONST, NFIRST = const_columns()
    NPAR = columns()[1]
    order = stream_order()

    with ExitStack() as ctx:
        counts = Counts(nc, ctx, known)
        tick, at = counts.tick, counts.at

        first, size, whole = {}, {}, {}
        b = 0
        for name, k in order:
            first[name], size[name] = b, k
            b += k
            whole[name] = b // BLK
        NSLOT = b // BLK
        groups = [name for name, _ in order]
        before = dict(zip(groups[1:], groups[:-1]))

        BASE = 16512
        state = [BASE]

        def place(name, shape, dt=F32):
            t = nc.alloc_sbuf_tensor_at(name, shape, dt, offset=state[0])
            state[0] += -(-4 * int(np.prod(shape[1:])) // 32) * 32
            return t

        XT = place("XT", [P, KC, T])
        AH_AT = state[0]
        AH = place("AH", [P, KC, T], F32R)
        AL = place("AL", [P, KC, T], F32R)
        RAWW = place("RAWW", [P, RAW, SLOT])
        WH = place("WH", [P, SPLIT, SLOT], F32R)
        WL = place("WL", [P, SPLIT, SLOT], F32R)
        CST_AT = state[0]
        CST = place("CST", [P, NFIRST])
        PAR_AT = state[0]
        PAR = place("PAR", [P, NPAR])
        PW_AT = state[0]
        PW = place("PW", [P, 2 * DEPTH, P])
        CT = place("CT", [P, KC, 2])
        C4 = place("C4", [P, KC, 4], F32R)
        MOD = place("MOD", [P, DEPTH, 48, 2])
        A1 = place("A1", [P, DEPTH, 2, KC, 2])
        SM = place("SM", [P, 256])
        SQ = place("SQ", [P, 2, T])
        RS = place("RS", [P, T])
        RR = place("RR", [P, T])
        TF = place("TF", [P, 2, T])
        REGION = state[0]

        HIDH = place("HIDH", [P, FC, T], F32R)
        HIDL = place("HIDL", [P, FC, T], F32R)
        assert state[0] <= 229376, state[0]
        END = state[0]

        state[0] = REGION
        QKN = place("QKN", [P, 8, T])
        VT = place("VT", [P, 4, 512])
        PX = place("PX", [P, 2, 2, T])
        AA = place("AA", [P, 2, T])
        AT = place("AT", [P, 2, T])
        ON = place("ON", [P, 4, 512])
        MIX = place("MIX", [P, KC, T])
        CP = place("CP", [P, 2, 2, S + 2 * PAD])
        CV = place("CV", [P, 2, T])
        UP = place("UP", [P, 2, 2, S + 2 * UPAD])
        PL = place("PL", [P, 2, T])
        QG = place("QG", [P, 2, T])
        ends = [state[0]]
        state[0] = REGION + 4 * (8 * T + 4 * 512)
        WA = place("WA", [P, 2, 2, S + 2 * UPAD])
        SGB = place("SGB", [P, 2, T])
        assert state[0] <= REGION + 4 * (8 * T + 4 * 512 + 8 * T)
        state[0] = REGION
        QN = place("QN", [P, 14, S])
        VA = place("VA", [P, 2, W2])
        VSW = place("VSW", [P, 2, 256])
        G = place("G", [P, 16, S])
        Y_AT = state[0]
        Y = place("Y", [P, 16, S])
        SG_AT = state[0]
        SG = place("SG", [P, 32, S])
        NS = place("NS", [P, 2, 384])
        CT2 = place("GT", [P, 64])
        ends.append(state[0])
        state[0] = REGION
        MH = place("MH", [P, KC, S], F32R)
        ML = place("ML", [P, KC, S], F32R)
        assert state[0] <= REGION + 4 * (14 * S + 2 * W2 + 512)
        state[0] = Y_AT
        CWV = place("CWV", [P, CMP_BLOCK, P])
        assert state[0] <= SG_AT
        state[0] = SG_AT
        CWK = place("CWK", [P, CMP_BLOCK, P])
        RGWS = place("RGWS", [P, 2048])
        XB = place("XB", [P, 4, S + 3])
        assert state[0] <= SG_AT + 4 * 32 * S
        state[0] = Y_AT - 4 * 8 * S
        KP = place("KP", [P, 2, CMP_BLOCK, 2 * NCMP])
        assert state[0] <= Y_AT
        state[0] = SG_AT
        LT = place("LT", [P, 4, S])
        MT = place("MT", [P, 2, 512])
        RG = RGWS[:, 0:1024].rearrange("p (g j e) -> p g j e", g=2, e=P)
        WS = RGWS[:, 1024:2048].rearrange("p (g t) -> p g t", t=P)
        state[0] = CST_AT + 4 * 512
        C2 = place("C2", [P, NCONST - NFIRST])
        W2KV = place("W2KV", [P, 2, DH])
        assert state[0] <= PAR_AT
        state[0] = PW_AT
        BS = place("BS", [P, 4, P])
        state[0] = AH_AT
        AHX = place("AHX", [P, KC, T])
        ALX = place("ALX", [P, KC, T])
        assert max(ends) <= 229376, (ends, END)

        B = [ctx.enter_context(nc.psum_tensor(f"bank{i}", [P, 512], F32)) for i in range(8)]
        MM, XX = (0, 1, 2, 3), (4, 5, 6, 7)
        uses = {}
        bank_of = {}
        turn = {MM: 0, XX: 0}

        def open_bank(pe, lane, name):
            b = lane[turn[lane] % len(lane)]
            turn[lane] += 1
            if b in uses:
                pe.wait_ge(*at(("free", b, uses[b])))
            uses[b] = uses.get(b, -1) + 1
            bank_of[name] = (b, uses[b])
            counts.found[("bank", name)] = (b, uses[b])
            return B[b]

        def bank(name):
            return B[counts.found.get(("bank", name), known.get(("bank", name), (0, 0)))[0]]

        def free(name, *products):
            b, n = counts.found.get(("bank", name), known.get(("bank", name), (0, 0)))
            for p in products:
                counts.found[p] = (f"bank{b}_read", n + 1)
            counts.found[("free", b, n)] = (f"bank{b}_read", n + 1)
            return counts.sem(f"bank{b}_read"), 1

        def par(n, j=0, w=1, rows=P):
            a = pc[n][0] + j
            return PAR[0:rows, a:a + w]

        def cst(n, j=0, w=None, rows=P):
            a = cc[n][0] + j
            if a >= NFIRST:
                return C2[0:rows, a - NFIRST:a - NFIRST + (cc[n][1] - j if w is None else w)]
            return CST[0:rows, a:a + (cc[n][1] - j if w is None else w)]

        def link(eng, name, ins):
            counts.n[name] = counts.n.get(name, 0) + 1
            ins.then_inc(counts.sem(name), 1)
            eng.wait_ge(counts.sem(name), counts.n[name])

        def streams(l):
            return (0, 1) if l == 0 else (1,)

        def cols(l):
            return slice(0, T) if l == 0 else slice(S, T)

        units = {l: [(s, q, h) for s in reversed(streams(l)) for q in range(2) for h in range(HEADS)]
                 for l in range(DEPTH)}
        tiles = {l: [(s, q) for s in reversed(streams(l)) for q in range(2)] for l in range(DEPTH)}

        filler = {0: [(0, g) for g in range(4, 12)] + [(1, g) for g in range(4)], 1: [(1, g) for g in range(4, 12)]}

        def half(pool, l, j, hf, w, win, st):
            r = slice(hf * DH, hf * DH + DH)
            o = UPAD - w // 2
            dst = PL[r, j, :].rearrange("p (s t) -> p s t", s=2)[:, st, :]
            n = st.stop - st.start
            ic = cst("icnt", j * S, S)[r, :].unsqueeze(1).to_broadcast([DH, n, S])
            link(pool, "pool_chain", pool.tensor_tensor(dst, win[:, :, o:o + S], ic, ALU.mult))
            ins = pool.tensor_tensor(dst, dst, UP[r, j, st, UPAD:UPAD + S], ALU.subtract)
            key = ("pl", l, j) if hf else ("pl_half", l, j)
            ins.then_inc(*tick("pool_means", key))
            pool.wait_ge(*at(key))

        def hidden_upper(act, l, j, cs):
            act.wait_ge(*at(("hf", l, j)))
            act.activation(HIDH[:, j, cs], TF[:, j % 2, cs], ACT.Identity).then_inc(*tick("operand_upper", ("hidh", l, j)))

        def hidden_left(l, j, cs):
            dve = nc.vector
            dve.wait_ge(*at(("hidh", l, j)))
            dve.tensor_tensor(HIDL[:, j, cs], TF[:, j % 2, cs], HIDH[:, j, cs].bitcast(F32), ALU.subtract) \
                .then_inc(*tick("hidden_ready", (("hid", l), j)))





        XS = slice(S, T)
        RUNS = [f"qa{c}" for c in range(4)] + [f"ka{c}" for c in range(4)] + [f"qc{c}" for c in range(4)] + ["ks0", "kw0"]
        GAINS = ["qna"] * 4 + ["kna"] * 4 + ["qnc"] * 4 + ["knc"] * 2
        UNITS = 24
        mg_after = [0] * UNITS
        for c in range(32):
            mg_after[c * UNITS // 32] += 1
        FG = RS[:, S:T]
        H1 = RR[:, S:S + 64].rearrange("p (w g c) -> p w g c", w=2, g=2)
        KCN = RR[:, S + 64:S + 80]
        VC = RR[0:NCMP, S + 80:S + 80 + P]
        PC = TF[:, :, 0:256].rearrange("p q (h c) -> p q h c", c=32)
        XC, RA = XT[:, 0:4, 0:S], XT[:, 4:8, 0:S]
        IG, UD = AHX[:, 0:4, 0:S], AHX[:, 4:8, 0:S]
        E2, VD = ALX[:, 0:4, 0:S], ALX[:, 4:8, 0:S]
        CROW, NROW = AHX[:, 0:4, 0:S], AHX[:, 4:8, 0:S]
        ACC = ALX[:, 0:4, 0:S]
        VBD = XT[:, 0:2, 0:S]
        PCT = XT[:, 2:4, 0:S]
        FT = NS[0:8].rearrange("p a b -> p (a b)")
        FL, FC_, FN = FT[:, 0:S], FT[:, S:2 * S], FT[:, 2 * S:3 * S]

        def pp(i, q):
            return XT[:, 4 + 2 * (i % 2) + q, 0:(q + 1) * P]


        GT = CT2
        MTF = TF

        def head_rows(i):
            b, h = divmod(i, 8)
            if b == 0:
                r = slice(h % 2 * DH, h % 2 * DH + DH)
                return QN[r, h // 2, :], QN[r, 4 + h // 2, :]
            r = slice(h // 4 * DH, h // 4 * DH + DH)
            return QN[r, 8 + h % 4, :], QN[r, 11 + b, :]

        def second_pe(pe, by_feature, by_token, sum_squares, transposes, product):
            sum_squares("n3", cst("ones"), KC, XS)

            def operand(name, fill="h3"):
                by_feature(name, fill, XS, S)

            for c, name in enumerate(RUNS):
                operand(name)
                if c:
                    sum_squares(("qk2", c - 1), cst("blk"), 1, slice(0, S))
            by_token("va", "h3", [S, S + P], W2)
            sum_squares(("qk2", 13), cst("blk"), 1, slice(0, S))
            by_token("vsw", "h3", [S, S + P], 256)
            for n in ("fg", "kcc", "vcc", "xb0", "xb1", "xb2", "xb3", "ud0", "ud1", "ud2", "ud3"):
                operand(n)
            by_token("vd", "h3", [S, S + P], W2)
            for w, cw in ((0, CWK), (1, CWV)):
                pe.wait_ge(*at(("kp", w)))
                pe.wait_ge(*at("cwk" if w == 0 else "cwv"))
                ps = open_bank(pe, XX, ("h1r", w))
                for k in range(CMP_BLOCK):
                    mm = pe.matmul(ps[0:2 * NCMP, 0:P], KP[:, w, k, :], cw[:, k, :], start=(k == 0), stop=(k == CMP_BLOCK - 1))
                mm.then_inc(*tick("compressed", ("h1r", w)))
                operand(f"G{w}")
                ps = open_bank(pe, XX, ("h1c", w))
                pe.wait_ge(*at(("h1rs", w)))
                transposes(ps, [RR[0:2 * NCMP, w * P:(w + 1) * P]], ("h1c", w))
            operand("G2")
            pe.wait_ge(*at("w2"))
            for w in range(2):
                ps = open_bank(pe, XX, ("c2", w))
                pe.wait_ge(*at(("h1s", w)))
                for g in range(2):
                    if w == 0:
                        mm = pe.matmul(ps[g * DH:(g + 1) * DH, 0:NCMP], W2KV[:, 0, :], H1[:, 0, g, 0:NCMP], start=True, stop=True)
                    else:
                        mm = pe.matmul(ps[0:NCMP, g * DH:(g + 1) * DH], H1[:, 1, g, 0:NCMP], W2KV[:, 1, :], start=True, stop=True)
                mm.then_inc(*tick("compressed", ("c2", w)))
            for c in range(3, 5):
                operand(f"G{c}")
            sum_squares("kcn", cst("blk"), 1, slice(0, NCMP))
            for c in range(5, 8):
                operand(f"G{c}")
            pe.wait_ge(*at("rgws"))
            for j in range(4):
                ps = open_bank(pe, XX, ("rg", j))
                pe.wait_ge(*at(("xc", j)))
                for g in range(2):
                    mm = pe.matmul(ps[:, g * S:(g + 1) * S], RG[:, g, j, :], XC[:, j, :], start=True, stop=True)
                mm.then_inc(*tick("recurrence_gates", ("rg", j)))
            operand("G8")
            operand("G9")
            pe.wait_ge(*at("ws_masked"))
            for q in range(2):
                ps = open_bank(pe, XX, ("sp", q))
                pe.wait_ge(*at(("vdn", q)))
                for g in range(8):
                    r = g % 2 * DH
                    mm = pe.matmul(ps[r:r + DH, g // 2 * P:(g // 2 + 1) * P], VD[:, 2 * q + g // 4, g % 4 * DH:(g % 4 + 1) * DH],
                                   WS[:, g, :], start=True, stop=True, skip_group_check=True)
                mm.then_inc(*tick("tokens_mixed", ("sp", q)))
            for c in range(10, 13):
                operand(f"G{c}")
            ps = open_bank(pe, XX, "gates")
            pe.wait_ge(*at("fg_gates"))
            for q in range(2):
                mm = pe.transpose(ps[:, q * 32:q * 32 + 24], FG[GATE_ROW:GATE_ROW + 24, q * P:(q + 1) * P],
                                  CST[GATE_ROW:GATE_ROW + 24, cc["ident"][0] + GATE_ROW:cc["ident"][0] + GATE_ROW + 24])
            mm.then_inc(*tick("transposes_done", "gates"))
            operand("G13")
            pe.wait_ge(*at("kcn_ready"))
            for q in range(2):
                for g in range(2):
                    ps = open_bank(pe, MM, ("cs", q, g))
                    r = slice(g * DH, g * DH + DH)
                    for h in range(4):
                        mm = pe.matmul(ps[:, h * 16:h * 16 + NCMP], QN[r, 8 + h, q * P:(q + 1) * P], KCN[r, 0:NCMP],
                                       start=True, stop=True)
                    mm.then_inc(*tick("scores_done", ("cs", q, g)))
            operand("G14")
            operand("G15")
            for q in range(2):
                ps = open_bank(pe, XX, ("cpT", q))
                pe.wait_ge(*at(("cp2", q)))
                transposes(ps, [TF[:, q, g * P:(g + 1) * P] for g in range(2)], ("cpT", q))
            for q in range(2):
                ps = open_bank(pe, XX, ("co", q))
                pe.wait_ge(*at(("cpTs", q)))
                pe.wait_ge(*at("vbd"))
                for g in range(2):
                    mm = pe.matmul(ps[:, g * 256:(g + 1) * 256], PCT[:, q, g * P:(g + 1) * P], VBD[:, g, :], start=True, stop=True)
                mm.then_inc(*tick("values_done", ("co", q)))

            def scores(i):
                qr, kr = head_rows(i)
                ps = open_bank(pe, MM, ("s2", i))
                fox = i < 8
                if i == 0:
                    pe.wait_ge(*at("rows_landed"))
                for c0, q, nk in ((0, 0, P), (P, 1, S)):
                    mm = pe.matmul(ps[:, c0:c0 + nk], qr[:, q * P:(q + 1) * P], kr[:, 0:nk], start=True, stop=not fox)
                    if fox:
                        r = i % 2 * DH
                        pe.matmul(ps[:, c0:c0 + nk], CROW[r:r + 1, i // 2, q * P:(q + 1) * P],
                                  C2[r:r + 1, cc["ones2"][0] - NFIRST:cc["ones2"][0] - NFIRST + nk], start=False, stop=False)
                        mm = pe.matmul(ps[:, c0:c0 + nk], C2[r:r + 1, cc["ones2"][0] - NFIRST:cc["ones2"][0] - NFIRST + P],
                                       NROW[r:r + 1, i // 2, 0:nk], start=False, stop=True)
                mm.then_inc(*tick("scores_done", ("s2", i)))

            def turned(i):
                ps = open_bank(pe, XX, ("pT2", i))
                pe.wait_ge(*at(("p2", i, 1)))
                transposes(ps, [pp(i, 0), pp(i, 1)[:, 0:P], pp(i, 1)[:, P:2 * P]], ("pT2", i))

            def values(i):
                b, h = divmod(i, 8)
                ps = open_bank(pe, XX, ("o2", i))
                pe.wait_ge(*at(("pTs", i)))
                pt = SQ[:, i % 2, :]
                v = [VA[:, t, h * DH:(h + 1) * DH] if b == 0 else VSW[:, t, (b - 1) * P + h // 4 * DH:(b - 1) * P + h // 4 * DH + DH]
                     for t in range(2)]
                pe.matmul(ps[:, 0:DH], pt[:, 0:P], v[0], start=True, stop=True)
                pe.matmul(ps[:, DH:2 * DH], pt[:, P:2 * P], v[0], start=True, stop=False)
                pe.matmul(ps[:, DH:2 * DH], pt[:, 2 * P:3 * P], v[1], start=False, stop=True) \
                    .then_inc(*tick("values_done", ("o2", i)))

            c = 0
            for i in range(UNITS + 2):
                if i < UNITS:
                    scores(i)
                if 1 <= i <= UNITS:
                    turned(i - 1)
                for _ in range(mg_after[i] if i < UNITS else 0):
                    operand(f"mg{c}")
                    c += 1
                if i >= 2:
                    values(i - 2)
                if i == 10:
                    for q in range(2):
                        ps = open_bank(pe, XX, ("yT", 0, q))
                        pe.wait_ge(*at(("fox", 7)))
                        transposes(ps, [MTF[:, q, j * P:(j + 1) * P] for j in range(4)], ("yT", 0, q))
            for q in range(2):
                ps = open_bank(pe, XX, ("yT", 2, q))
                pe.wait_ge(*at(("nsa", UNITS - 1)))
                transposes(ps, [ACC[:, 2 * q + j // 2, j % 2 * P:(j % 2 + 1) * P] for j in range(4)], ("yT", 2, q))
            for d in range(8):
                for n in range(4):
                    name = f"br{d}_{n}"
                    ps = open_bank(pe, MM, name)[:, 0:S]
                    product(name, [ps], lambda kb, n=n: pe.wait_ge(*at(("y_operand", (4 * n + kb) // 2))),
                            lambda kb, t, n=n: tuple(x[:, (4 * n + kb) // 2, (4 * n + kb) % 2 * S:(4 * n + kb) % 2 * S + S] for x in (AH, AL)), S)
            for d in range(8):
                by_feature(f"wo{d}.2", "merged", slice(0, S), S, (MH, ML))

        def second_act(act, square, root):
            for kc in range(KC):
                act.wait_ge(*at(("x", "fo", DEPTH - 1, kc, 1)))
                square(XT[:, kc, XS], XS)
            act.wait_ge(*at(("mm", "fo7.1", 0)))
            for n, dst, key in (("rg_ws", RGWS[:], "rgws"), ("bs", BS[:].rearrange("p a b -> p (a b)"), "bs"),
                                ("w1k", CWK[:].rearrange("p a b -> p (a b)"), "cwk"),
                                ("w1v", CWV[:].rearrange("p a b -> p (a b)"), "cwv"),
                                ("w2", W2KV[:].rearrange("p a b -> p (a b)"), "w2")):
                a, w = EXTRA[n]
                act.dma_start(dst, io["extra"][:, a:a + w]).then_inc(*tick(f"{key}_landed", key, by=16))
            act.dma_start(C2[:], io["cst"][:, NFIRST:NCONST]).then_inc(*tick("c2_landed", "c2", by=16))
            root("n3", RS, S, 1.0 / D)

            def head_evac(c):
                act.wait_ge(*at(("mm", RUNS[c], 0)))
                square(bank(RUNS[c])[:, 0:S], slice(0, S))
                g = SM[:, 128:129] if c < 4 else SM[:, 129:130] if 8 <= c < 12 else par(GAINS[c])
                act.activation(QN[:, c, :], bank(RUNS[c])[:, 0:S], ACT.Identity, scale=g).then_inc(*free(RUNS[c], ("qn_raw", c)))

            def head_root(c):
                act.wait_ge(*at(("rr_2", c - 1) if c else "rr3"))
                root(("qk2", c), RS, S, 1.0 / DH)

            act.wait_ge(*at("gains2"))
            act.wait_ge(*at("lam_abs"))
            act.activation(SM[:, 152:156], SM[:, 152:156], ACT.Exp).then_inc(*tick("softplus_exps", "lam_exp"))
            for c in range(14):
                head_evac(c)
                if c:
                    head_root(c - 1)
            for t in range(2):
                act.wait_ge(*at(("mm", "va", t)))
                act.activation(VA[:, t, :], bank(("va", t))[:], ACT.Copy).then_inc(*free(("va", t), ("va", t)))
            head_root(13)
            for t in range(2):
                act.wait_ge(*at(("mm", "vsw", t)))
                act.activation(VSW[:, t, :], bank(("vsw", t))[:, 0:256], ACT.Copy).then_inc(*free(("vsw", t), ("vsw", t)))
            act.wait_ge(*at(("mm", "fg", 0)))
            act.activation(FG[0:8, :], bank("fg")[0:8, 0:S], ACT.Identity, bias=par("bf", 0, 1, 8)).then_inc(*tick("f_logits", "fg_f"))
            act.activation(FG[GATE_ROW:GATE_ROW + 24, :], bank("fg")[GATE_ROW:GATE_ROW + 24, 0:S], ACT.Sigmoid) \
                .then_inc(*free("fg", "fg_gates"))
            for j in range(4):
                act.wait_ge(*at(("mm", f"xb{j}", 0)))
                act.activation(XB[:, j, 3:3 + S], bank(f"xb{j}")[:, 0:S], ACT.Copy).then_inc(*free(f"xb{j}", ("xb", j)))
            for j in range(4):
                act.wait_ge(*at(("mm", f"ud{j}", 0)))
                act.activation(UD[:, j, :], bank(f"ud{j}")[:, 0:S], ACT.Gelu).then_inc(*free(f"ud{j}", ("ud", j)))
            for t in range(2):
                act.wait_ge(*at(("mm", "vd", t)))
                act.activation(VD[:, 2 * t:2 * t + 2, :], bank(("vd", t))[:].rearrange("p (a b) -> p a b", b=S), ACT.Gelu,
                               accum_out=SM[:, 132 + t:133 + t]).then_inc(*free(("vd", t), ("vd", t)))
            for w in range(2):
                act.wait_ge(*at(("h1r", w)))
                act.wait_ge(*at(("qn", 13)))
                act.activation(RR[0:2 * NCMP, w * P:(w + 1) * P], bank(("h1r", w))[0:2 * NCMP, 0:P], ACT.Copy) \
                    .then_inc(*free(("h1r", w), ("h1rs", w)))
                gate(act, w)
                act.wait_ge(*at(("h1c", w)))
                act.activation(H1[:, w, :, 0:NCMP], bank(("h1c", w))[:, 0:2 * NCMP].rearrange("p (g c) -> p g c", g=2), ACT.Silu) \
                    .then_inc(*free(("h1c", w), ("h1s", w)))
            gate(act, 2)
            act.wait_ge(*at(("c2", 0)))
            square(bank(("c2", 0))[:, 0:NCMP], slice(0, NCMP))
            act.activation(KCN[:, 0:NCMP], bank(("c2", 0))[:, 0:NCMP], ACT.Identity, scale=par("knc")).then_inc(*free(("c2", 0), "kc_raw"))
            act.wait_ge(*at(("c2", 1)))
            act.activation(VC, bank(("c2", 1))[0:NCMP, 0:P], ACT.Copy).then_inc(*free(("c2", 1), "vc"))
            for c in range(3, 5):
                gate(act, c)
            act.wait_ge(*at(("rr_2", 13)))
            root("kcn", RS, NCMP, 1.0 / DH)
            for t in range(2):
                act.wait_ge(*at(("vdc", t)))
                act.activation(NS[:].rearrange("p a b -> p (a b)")[:, 0:512].rearrange("p (a b) -> p a b", b=S), VD[:, 2 * t:2 * t + 2, :],
                               ACT.Square, accum_out=SM[:, 134 + t:135 + t]).then_inc(*tick("token_squares", ("vds", t)))
                act.wait_ge(*at(("vds", t)))
            act.activation(SM[:, 136:138], SM[:, 134:136], ACT.Sqrt, bias=SM[:, 8:9], scale=1.0 / W2).then_inc(*tick("token_roots", "vdroot"))
            for c in range(5, 8):
                gate(act, c)
            for j in range(4):
                act.wait_ge(*at(("rg", j)))
                act.activation(RA[:, j, :], bank(("rg", j))[:, 0:S], ACT.Sigmoid, bias=par("bra", j)).then_inc(*tick("r_ready", ("r", j)))
                act.activation(IG[:, j, :], bank(("rg", j))[:, S:T], ACT.Sigmoid, bias=par("brx", j)).then_inc(*free(("rg", j), ("ig", j)))
            for c in (8, 9):
                gate(act, c)
            act.wait_ge(*at("softplus"))
            for j in range(4):
                act.wait_ge(*at(("r", j)))
                act.activation(E2[:, j, :], RA[:, j, :], ACT.Exp, scale=SM[:, 144 + j:145 + j]).then_inc(*tick("decay", ("e2", j)))
                act.activation(LT[:, j, :], RA[:, j, :], ACT.Tanh, scale=SM[:, 148 + j:149 + j]).then_inc(*tick("decay", ("th", j)))
                act.wait_ge(*at(("th", j)))
                act.activation(RA[:, j, :], RA[:, j, :], ACT.Exp, scale=SM[:, 140 + j:141 + j]).then_inc(*tick("decay", ("a", j)))
            act.wait_ge(*at("f_abs"))
            act.wait_ge(*at("b_square"))
            act.activation(LT[:], LT[:], ACT.Sqrt).then_inc(*tick("decay", "b_root"))
            for c in (10, 11, 12):
                gate(act, c)
            act.activation(FL, FL, ACT.Exp, scale=-1.0).then_inc(*tick("f_terms", "f_exp"))
            act.wait_ge(*at("f_exp"))
            act.activation(FL, FL, ACT.Ln, bias=1.0).then_inc(*tick("f_terms", "f_log"))
            gate(act, 13)
            act.wait_ge(*at("c_rows"))
            for h in range(8):
                for src, dst in ((FC_[h:h + 1, :], CROW), (FN[h:h + 1, :], NROW)):
                    act.dma_start(dst[h % 2 * DH:h % 2 * DH + 1, h // 2, :], src) \
                        .then_inc(*tick("rows_landed", *(["rows_landed"] if h == 7 and dst is NROW else []), by=16))
            for c in (14, 15):
                gate(act, c)
            for q in range(2):
                act.wait_ge(*at(("cd2", q)))
                act.activation(PC[:, q, :, 0:NCMP], PC[:, q, :, 0:NCMP], ACT.Exp).then_inc(*tick("compressed_probs", ("cexp", q)))
            for q in range(2):
                act.wait_ge(*at(("cpT", q)))
                act.activation(PCT[:, q, :], bank(("cpT", q))[:, 0:256], ACT.Copy).then_inc(*free(("cpT", q), ("cpTs", q)))

            c = 0
            for i in range(UNITS + 1):
                if i < UNITS:
                    act.wait_ge(*at(("nm2", i)))
                    if i >= 2:
                        act.wait_ge(*at(("pT2", i - 2)))
                    o = 160 + 4 * (i % 4)
                    for q, c0, c1 in ((0, 0, P), (1, P, 384)):
                        act.activation(pp(i, q), NS[:, i % 2, c0:c1], ACT.Exp, scale=-1.0, bias=SM[:, o + q:o + q + 1],
                                       accum_out=SM[:, 176 + 2 * i + q:177 + 2 * i + q]).then_inc(*tick("probs_ready", ("p2", i, q)))
                if i >= 1:
                    act.wait_ge(*at(("pT2", i - 1)))
                    if i >= 3:
                        act.wait_ge(*at(("o2", i - 3)))
                    act.activation(SQ[:, (i - 1) % 2, 0:384], bank(("pT2", i - 1))[:, 0:384], ACT.Copy).then_inc(*free(("pT2", i - 1), ("pTs", i - 1)))
                for _ in range(mg_after[i] if i < UNITS else 0):
                    act.wait_ge(*at(("mm", f"mg{c}", 0)))
                    if c == 0:
                        act.wait_ge(*at(("ys", 1)))
                    act.activation(SG[:, c, :], bank(f"mg{c}")[:, 0:S], ACT.Copy).then_inc(*free(f"mg{c}", ("mg", c)))
                    c += 1
            act.wait_ge(*at(("mg", 31)))
            for d in range(8):
                v = SG[:, d:32:8, :]
                act.activation(v, v, ACT.Sigmoid).then_inc(*tick("merge_gates", ("sg", d)))
            act.wait_ge(*at(("mm", "mg31", 0)))
            for j in (2, 3, 6, 7, 0, 1, 4, 5):
                act.wait_ge(*at(("y_full", j // 2)))
                act.activation(AH[:, j, :], Y[:, 2 * j:2 * j + 2, :].rearrange("p a b -> p (a b)"), ACT.Identity) \
                    .then_inc(*tick("operand_upper", ("ahy", j)))
            for d in range(8):
                act.wait_ge(*at(("m_full", d)))
                act.activation(MH[:, d, :], TF[:, d % 2, 0:S], ACT.Identity).then_inc(*tick("operand_upper", ("mh", d)))

        def gate(act, c):
            act.wait_ge(*at(("mm", f"G{c}", 0)))
            act.activation(G[:, c, :], bank(f"G{c}")[:, 0:S], ACT.Silu).then_inc(*free(f"G{c}", ("G", c)))

        def second_dve(dve, weights, L, reciprocal_root):
            L(dve.tensor_scalar(SM[:, 128:129], par("qna"), DH ** -0.5, None, ALU.mult))
            dve.tensor_scalar(SM[:, 129:130], par("qnc"), DH ** -0.5, None, ALU.mult).then_inc(*tick("gains2", "gains2"))
            weights("qa0")
            reciprocal_root("n3", S, "rr3")
            for kc in range(KC):
                if kc >= 2:
                    dve.wait_ge(*at(("h3", kc - 2)))
                dve.scalar_tensor_tensor(out=TF[:, kc % 2, 0:S], in0=XT[:, kc, XS], scalar=par("ng2", kc), in1=RR[:, 0:S],
                                         op0=ALU.mult, op1=ALU.mult).then_inc(*tick("normed", ("h3f", kc)))
                dve.wait_ge(*at(("h3f", kc)))
                L(dve.tensor_copy(AH[:, kc, XS], TF[:, kc % 2, 0:S]))
                dve.tensor_tensor(AL[:, kc, XS], TF[:, kc % 2, 0:S], AH[:, kc, XS].bitcast(F32), ALU.subtract) \
                    .then_inc(*tick("operand_ready", ("h3", kc)))
            lam, e, z, z2, acc = par("lam", 0, 4), SM[:, 152:156], SM[:, 156:160], SM[:, 232:236], SM[:, 236:240]
            dve.scalar_tensor_tensor(out=e, in0=lam, scalar=-1.0, in1=lam, op0=ALU.mult, op1=ALU.min).then_inc(*tick("softplus_terms", "lam_abs"))

            def head(c):
                reciprocal_root(("qk2", c), S, ("rr_2", c))
                dve.wait_ge(*at(("qn_raw", c)))
                dve.tensor_tensor(QN[:, c, :], QN[:, c, :], RR[:, 0:S], ALU.mult).then_inc(*tick("heads_ready", ("qn", c)))
                dve.wait_ge(*at(("qn", c)))

            for c in range(14):
                weights(RUNS[c])
                if c:
                    head(c - 1)
            weights("va")
            head(13)
            weights("vsw")
            L(dve.memset(XB[:, :, 0:3], 0.0))
            L(dve.memset(KP[:], 0.0))
            for n in ("fg", "kcc", "vcc"):
                weights(n)
            for w, n in ((0, "kcc"), (1, "vcc")):
                dve.wait_ge(*at(("mm", n, 0)))
                src = bank(n)[:, 0:S].rearrange("p (c a) -> p a c", a=16)
                pos = par("pos", 0, CMP_BLOCK).unsqueeze(2).to_broadcast([P, CMP_BLOCK, NCMP])
                for g in range(2):
                    h = slice(g * DH, g * DH + DH)
                    c = slice(g * NCMP, (g + 1) * NCMP)
                    L(dve.tensor_tensor(KP[h, w, 0:16, c], src[h, :, 0:NCMP], pos[h, 0:16, :], ALU.add))
                    ins = dve.tensor_tensor(KP[h, w, 16:32, c], src[h, :, 1:NCMP + 1], pos[h, 16:32, :], ALU.add)
                    if g == 0:
                        L(ins)
                    else:
                        ins.then_inc(*free(n, ("kp", w)))
            for n in ("xb0", "xb1", "xb2", "xb3"):
                weights(n)
            dve.wait_ge(*at("lam_exp"))
            L(dve.tensor_scalar(z, e, 2.0, None, ALU.add))
            L(dve.reciprocal(z, z))
            L(dve.tensor_tensor(z, z, e, ALU.mult))
            L(dve.tensor_tensor(z2, z, z, ALU.mult))
            L(dve.memset(acc, 1.0 / 19))
            for k in range(17, 0, -2):
                L(dve.tensor_tensor(acc, acc, z2, ALU.mult))
                L(dve.tensor_scalar(acc, acc, 1.0 / k, None, ALU.add))
            L(dve.tensor_tensor(acc, acc, z, ALU.mult))
            L(dve.tensor_scalar(z, lam, -1.0, 0.0, ALU.mult, ALU.max))
            L(dve.scalar_tensor_tensor(out=z, in0=acc, scalar=2.0, in1=z, op0=ALU.mult, op1=ALU.add))
            L(dve.tensor_scalar(SM[:, 140:144], z, -LRU_C, None, ALU.mult))
            L(dve.tensor_scalar(SM[:, 144:148], z, -2 * LRU_C, None, ALU.mult))
            dve.tensor_scalar(SM[:, 148:152], z, LRU_C, None, ALU.mult).then_inc(*tick("softplus", "softplus"))
            for n in ("ud0", "ud1"):
                weights(n)

            def conv4(j):
                dve.wait_ge(*at(("xb", j)))
                for k in range(4):
                    w = par("w4", 4 * j + k)
                    if k == 0:
                        L(dve.tensor_scalar(XC[:, j, :], XB[:, j, 0:S], w, par("b4", j), ALU.mult, ALU.add))
                    else:
                        ins = dve.scalar_tensor_tensor(out=XC[:, j, :], in0=XB[:, j, k:k + S], scalar=w, in1=XC[:, j, :],
                                                       op0=ALU.mult, op1=ALU.add)
                        if k < 3:
                            L(ins)
                        else:
                            ins.then_inc(*tick("convolved", ("xc", j)))
                            dve.wait_ge(*at(("xc", j)))

            conv4(0)
            weights("ud2")
            conv4(1)
            weights("ud3")
            conv4(2)
            weights("vd")
            conv4(3)
            weights("G0")
            weights("G1")
            weights("G2")
            for t in range(2):
                dve.wait_ge(*at(("vd", t)))
                L(dve.tensor_scalar(SM[:, 138:139], SM[:, 132 + t:133 + t], -1.0 / W2, None, ALU.mult))
                dve.tensor_scalar(VD[:, 2 * t:2 * t + 2, :], VD[:, 2 * t:2 * t + 2, :], SM[:, 138:139], None, ALU.add) \
                    .then_inc(*tick("token_centred", ("vdc", t)))
                dve.wait_ge(*at(("vdc", t)))
            for c in range(3, 5):
                weights(f"G{c}")
            weights("G5")
            dve.wait_ge(*at(("root", "kcn")))
            L(dve.reciprocal(RR[:, 0:NCMP], RS[:, 0:NCMP]))
            dve.wait_ge(*at("kc_raw"))
            dve.tensor_tensor(KCN[:, 0:NCMP], KCN[:, 0:NCMP], RR[:, 0:NCMP], ALU.mult).then_inc(*tick("heads_ready", "kcn_ready"))
            dve.wait_ge(*at("kcn_ready"))
            weights("G6")
            weights("G7")
            dve.wait_ge(*at("vdroot"))
            L(dve.reciprocal(SM[:, 136:138], SM[:, 136:138]))
            for t in range(2):
                dve.tensor_scalar(VD[:, 2 * t:2 * t + 2, :], VD[:, 2 * t:2 * t + 2, :], SM[:, 136 + t:137 + t], None, ALU.mult) \
                    .then_inc(*tick("token_normed", ("vdn", t)))
            weights("G8")
            weights("G9")
            dve.wait_ge(*at("fg_f"))
            dve.scalar_tensor_tensor(out=FL, in0=FG[0:8, :], scalar=-1.0, in1=FG[0:8, :], op0=ALU.mult, op1=ALU.max).then_inc(*tick("f_abs", "f_abs"))
            for j in range(4):
                dve.wait_ge(*at(("e2", j)))
                dve.wait_ge(*at(("th", j)))
            dve.scalar_tensor_tensor(out=LT[:], in0=E2, scalar=1.0, in1=LT[:], op0=ALU.add, op1=ALU.mult) \
                .then_inc(*tick("recurrence", "b_square"))
            dve.wait_ge(*at(("ig", 3)))
            L(dve.tensor_tensor(IG, IG, XC, ALU.mult))
            weights("G10")
            dve.wait_ge(*at("b_root"))
            L(dve.tensor_tensor(LT[:], LT[:], IG, ALU.mult))
            for j in range(4):
                dve.wait_ge(*at(("a", j)))
                L(dve.tensor_tensor_scan(E2[:, j, :], RA[:, j, :], LT[:, j, :], 0.0, ALU.mult, ALU.add))
            weights("G11")
            for j in range(4):
                dve.wait_ge(*at(("G", 7)))
                dve.tensor_tensor(Y[:, 4 + j, :], E2[:, j, :], G[:, 4 + j, :], ALU.mult) \
                    .then_inc(*tick("branches", *([("y_full", 1)] if j == 3 else [("yb", j)])))
            weights("G12")
            weights("G13")
            dve.wait_ge(*at("f_log"))
            dve.wait_ge(*at("c2"))
            L(dve.scalar_tensor_tensor(out=FL, in0=FG[0:8, :], scalar=0.0, in1=FL, op0=ALU.min, op1=ALU.subtract))
            L(dve.tensor_tensor_scan(FC_, cst("ones2", 0, S, 8), FL, 0.0, ALU.mult, ALU.add))
            L(dve.tensor_scalar(FN, FC_, -1.0, None, ALU.mult))
            dve.wait_ge(*at("bs"))
            for q in range(2):
                dve.wait_ge(*at(("sp", q)))
                for j in range(4):
                    ins = dve.scalar_tensor_tensor(out=MT[:, q, j * P:(j + 1) * P], in0=bank(("sp", q))[:, j * P:(j + 1) * P],
                                                   scalar=par("lnv", j), in1=BS[:, j, :], op0=ALU.mult, op1=ALU.add)
                    if j < 3:
                        L(ins)
                    else:
                        ins.then_inc(*free(("sp", q), ("spe", q)))
                        dve.wait_ge(*at(("spe", q)))
                mt = MT[:, q, :].rearrange("p (a b) -> p a b", b=P)
                L(dve.tensor_tensor(mt, mt, UD[:, :, q * P:(q + 1) * P], ALU.mult))
            dve.memset(SM[:, 254:255], 0.0).then_inc(*tick("c_rows", "c_rows"))
            weights("G14")
            dve.wait_ge(*at("gates"))
            for q in range(2):
                ins = dve.tensor_copy(GT[:, 32 * q:32 * q + 24], bank("gates")[:, 32 * q:32 * q + 24])
                if q:
                    ins.then_inc(*free("gates", "gt"))
                    dve.wait_ge(*at("gt"))
                else:
                    L(ins)
            L(dve.memset(TF[:, :, 0:256], 0.0))
            L(dve.memset(VBD, 0.0))
            dve.wait_ge(*at("vc"))
            for g in range(2):
                for h in range(4):
                    ins = dve.tensor_copy(VBD[32 * h:32 * h + NCMP, g, h * DH:(h + 1) * DH], VC[:, g * DH:(g + 1) * DH])
                    if (g, h) == (1, 3):
                        ins.then_inc(*tick("compressed_values", "vbd"))
                        dve.wait_ge(*at("vbd"))
                    else:
                        L(ins)

            def bc(ap, n):
                return ap.unsqueeze(2).to_broadcast([P, ap.shape[1], n])

            for q in range(2):
                pq = PC[:, q, :, 0:NCMP]
                m = cst("cmpm", 16 * q, NCMP).unsqueeze(1).to_broadcast([P, 4, NCMP])
                for g in range(2):
                    dve.wait_ge(*at(("cs", q, g)))
                    ins = dve.tensor_tensor(PC[:, q, 4 * g:4 * g + 4, 0:NCMP], bank(("cs", q, g))[:, 0:64].rearrange("p (h c) -> p h c", c=16)[:, :, 0:NCMP],
                                            m, ALU.add)
                    ins.then_inc(*free(("cs", q, g), ("csm", q, g)))
                    dve.wait_ge(*at(("csm", q, g)))
                L(dve.tensor_reduce(SM[:, 224:232], pq, AX.X, ALU.max))
                dve.tensor_tensor(pq, pq, bc(SM[:, 224:232], NCMP), ALU.subtract).then_inc(*tick("compressed_centred", ("cd2", q)))
                dve.wait_ge(*at(("cexp", q)))
                L(dve.tensor_reduce(SM[:, 224:232], pq, AX.X, ALU.add))
                L(dve.reciprocal(SM[:, 224:232], SM[:, 224:232]))
                L(dve.tensor_tensor(pq, pq, bc(SM[:, 224:232], NCMP), ALU.mult))
                ok = cst("cmp01", 16 * q, NCMP).unsqueeze(1).to_broadcast([P, 8, NCMP])
                dve.tensor_tensor(pq, pq, ok, ALU.mult).then_inc(*tick("compressed_probs_ready", ("cp2", q)))
            weights("G15")
            for q in range(2):
                mt = MT[:, q, :].rearrange("p (a b) -> p a b", b=P)
                dve.wait_ge(*at(("G", 15)))
                dve.tensor_tensor(Y[:, 12:16, q * P:(q + 1) * P], mt, G[:, 12:16, q * P:(q + 1) * P], ALU.mult) \
                    .then_inc(*tick("branches", *([("y_full", 3), ("ys", 1)] if q else [("ys", 0)])))
            for q in range(2):
                dve.wait_ge(*at(("co", q)))
                for g in range(2):
                    gg = bc(GT[:, q * 32 + 4 * g:q * 32 + 4 * g + 4], DH)
                    ins = dve.tensor_tensor(ACC[:, 2 * q + g, :].rearrange("p (h e) -> p h e", e=DH),
                                            bank(("co", q))[:, g * 256:(g + 1) * 256].rearrange("p (h e) -> p h e", e=DH), gg, ALU.mult)
                    if g:
                        ins.then_inc(*free(("co", q), ("acc0", q)))
                        dve.wait_ge(*at(("acc0", q)))
                    else:
                        L(ins)

            def masked(i):
                dve.wait_ge(*at(("s2", i)))
                if i < 2:
                    dve.wait_ge(*at("rows_landed"))
                if i >= 2:
                    dve.wait_ge(*at(("p2", i - 2, 1)))
                o = 160 + 4 * (i % 4)
                for q, c0, c1 in ((0, 0, P), (1, P, 384)):
                    ins = dve.tensor_tensor_reduce(NS[:, i % 2, c0:c1], bank(("s2", i))[:, c0:c1], cst("cmask", c0, c1 - c0), -1.0, 3.0e38,
                                                   ALU.add, ALU.min, SM[:, o + q:o + q + 1])
                    if q:
                        ins.then_inc(*free(("s2", i), ("nm2", i)))
                        dve.wait_ge(*at(("nm2", i)))
                    else:
                        L(ins)

            def output(i):
                b, h = divmod(i, 8)
                o = 224 + 2 * (i % 4)
                dve.wait_ge(*at(("p2", i, 1)))
                L(dve.reciprocal(SM[:, o:o + 2], SM[:, 176 + 2 * i:178 + 2 * i]))
                if b:
                    L(dve.tensor_tensor(SM[:, o:o + 2], SM[:, o:o + 2], GT[:, 8 * b + h:8 * b + h + 33:32], ALU.mult))
                dve.wait_ge(*at(("o2", i)))
                src = bank(("o2", i))[:, 0:P].rearrange("p (q e) -> p q e", e=DH)
                if b == 0:
                    if h == 0:
                        dve.wait_ge(*at(("cpTs", 1)))
                    dve.tensor_tensor(MTF[:, :, h * DH:(h + 1) * DH], src, bc(SM[:, o:o + 2], DH), ALU.mult) \
                        .then_inc(*free(("o2", i), ("fox", h)))
                    dve.wait_ge(*at(("fox", h)))
                else:
                    t = RR[:, 0:P].rearrange("p (q e) -> p q e", e=DH)
                    dve.tensor_tensor(t, src, bc(SM[:, o:o + 2], DH), ALU.mult).then_inc(*free(("o2", i), ("ot", i)))
                    dve.wait_ge(*at(("ot", i)))
                    a = ACC[:, h // 4:h // 4 + 3:2, h % 4 * DH:(h % 4 + 1) * DH]
                    dve.tensor_tensor(a, a, t, ALU.add).then_inc(*tick("nsa_sums", ("nsa", i)))
                    dve.wait_ge(*at(("nsa", i)))

            def gated(b):
                for q in range(2):
                    dve.wait_ge(*at(("yT", b, q)))
                    dve.tensor_tensor(Y[:, 4 * b:4 * b + 4, q * P:(q + 1) * P], bank(("yT", b, q))[:].rearrange("p (a b) -> p a b", b=P),
                                      G[:, 4 * b:4 * b + 4, q * P:(q + 1) * P], ALU.mult) \
                        .then_inc(*free(("yT", b, q), *([("y_full", b)] if q else [("yg", b)])))

            c = 0
            for i in range(UNITS + 2):
                if i < UNITS:
                    masked(i)
                    for _ in range(mg_after[i]):
                        weights(f"mg{c}")
                        c += 1
                if i >= 2:
                    output(i - 2)
                if i == 10:
                    gated(0)
            gated(2)
            weights("br0_0")
            for j in (2, 3, 6, 7, 0, 1, 4, 5):
                dve.wait_ge(*at(("ahy", j)))
                dve.tensor_tensor(AL[:, j, :], Y[:, 2 * j:2 * j + 2, :].rearrange("p a b -> p (a b)"), AH[:, j, :].bitcast(F32), ALU.subtract) \
                    .then_inc(*tick("operand_ready", ("y_operand", j)))
            for d in range(8):
                for n in range(4):
                    name = f"br{d}_{n}"
                    weights(name)
                    dve.wait_ge(*at(("mm", name, 0)))
                    if n == 0:
                        dve.wait_ge(*at(("sg", d)))
                        if d >= 2:
                            dve.wait_ge(*at(("merged", d - 2)))
                    dst = TF[:, d % 2, 0:S] if n == 0 else RR[:, 0:S]
                    dve.tensor_tensor(dst, bank(name)[:, 0:S], SG[:, 8 * n + d, :], ALU.mult).then_inc(*free(name, ("bp", d, n)))
                    dve.wait_ge(*at(("bp", d, n)))
                    if n:
                        ins = dve.tensor_tensor(TF[:, d % 2, 0:S], TF[:, d % 2, 0:S], RR[:, 0:S], ALU.add)
                        if n == 3:
                            ins.then_inc(*tick("merged_full", ("m_full", d)))
                        else:
                            L(ins)
                if d:
                    merged_left(dve, d - 1)
            weights("wo0.2")
            merged_left(dve, 7)
            for d in range(8):
                if d:
                    weights(f"wo{d}.2")
                dve.wait_ge(*at(("mm", f"wo{d}.2", 0)))
                dve.tensor_tensor(XT[:, d, XS], XT[:, d, XS], bank(f"wo{d}.2")[:, 0:S], ALU.add).then_inc(*free(f"wo{d}.2", ("out", d)))

        def merged_left(dve, d):
            dve.wait_ge(*at(("mh", d)))
            dve.tensor_tensor(ML[:, d, :], TF[:, d % 2, 0:S], MH[:, d, :].bitcast(F32), ALU.subtract) \
                .then_inc(*tick("merged_ready", ("merged", d)))

        block = ctx.enter_context(nc.Block())

        @block.tensor
        def _(pe):
            squares = [0]

            def product(name, banks, acts, rhs_of, n, wide=False):
                b0, k = first[name], size[name]
                per = n // P if wide else 1
                for kb in range(k // per):
                    b = b0 + kb * per
                    slot = b // BLK
                    i = slot
                    if b % BLK == 0 or kb == 0:
                        pe.wait_ge(*at(("lo", i)))
                    o = b % BLK * P
                    w = [x[:, i % SPLIT, o:o + (n if wide else P)] for x in (WH, WL)]
                    acts(kb)
                    last_of_slot = (b + per) % BLK == 0
                    for t, ps in enumerate(banks):
                        hi, lo = rhs_of(kb, t)
                        pairs = [(w[0], hi), (w[0], lo), (w[1], hi)]
                        for j, (a, c) in enumerate(pairs):
                            if wide:
                                a, c = c, a
                            mm = pe.matmul(ps, a, c, start=(kb == 0 and j == 0), stop=(kb == k // per - 1 and j == 2))
                        keys = []
                        if last_of_slot and t == len(banks) - 1:
                            keys.append(("slot", i))
                        if kb == k // per - 1:
                            keys.append(("mm", name, t))
                        if keys:
                            mm.then_inc(*tick("products_done", *keys))

            def by_feature(name, fill, cs, n, src=None):
                ps = open_bank(pe, MM, name)[:, 0:n]
                hi, lo = src or (AH, AL)

                def acts(kb):
                    pe.wait_ge(*at((fill, kb)))
                product(name, [ps], acts, lambda kb, t: (hi[:, kb, cs], lo[:, kb, cs]), n)

            def by_token(name, fill, tile_cols, n):
                banks = [open_bank(pe, MM, (name, t))[:, 0:n] for t in range(len(tile_cols))]

                def acts(kb):
                    pe.wait_ge(*at((fill, kb)))
                product(name, banks, acts, lambda kb, t: (AH[:, kb, tile_cols[t]:tile_cols[t] + P],
                                                          AL[:, kb, tile_cols[t]:tile_cols[t] + P]), n, wide=True)

            def sum_squares(name, lhs, n_terms, cs):
                ps = open_bank(pe, XX, name)
                n = cs.stop - cs.start
                for k in range(n_terms):
                    q = squares[0]
                    pe.wait_ge(*at(("sq", q)))
                    pe.matmul(ps[:, 0:n], lhs, SQ[:, q % 2, cs], start=(k == 0), stop=(k == n_terms - 1)) \
                        .then_inc(*tick("squares_used", ("sq_used", q), *([("sum", name)] if k == n_terms - 1 else [])))
                    squares[0] += 1

            def modulation(l, g):
                name = f"mod{g}.{l}"
                ps = open_bank(pe, MM, name)
                pe.wait_ge(*at("c_left"))
                for kb in range(KC):
                    slot = first[name] // BLK + kb // 2
                    if kb % 2 == 0:
                        pe.wait_ge(*at(("lo", slot)))
                    o = kb % 2 * 512
                    for j, x in enumerate((WH, WL)):
                        mm = pe.matmul(ps[0:4, :], C4[:, kb, :], x[:, slot % SPLIT, o:o + 512], start=(kb == 0 and j == 0),
                                       stop=(kb == KC - 1 and j == 1))
                    if kb % 2:
                        mm.then_inc(*tick("products_done", ("slot", slot), *([("mm", name, 0)] if kb == KC - 1 else [])))

            def modulation_turned(l, g):
                ps = open_bank(pe, XX, ("modT", l, g))
                pe.wait_ge(*at(("mod_rows", l, g)))
                for j in range(4):
                    mm = pe.matmul(ps[:, 2 * j:2 * j + 2], TF[0:4, g % 2, j * P:(j + 1) * P], cst("pair", 0, 2, 4),
                                   start=True, stop=True)
                mm.then_inc(*tick("modulation_done", ("modT", l, g)))

            def transposes(ps, pieces, *keys):
                for j, piece in enumerate(pieces):
                    n = piece.shape[0]
                    mm = pe.transpose(ps[0:piece.shape[1], j * P:j * P + n], piece, cst("ident", 0, n, n))
                mm.then_inc(*tick("transposes_done", *keys))

            pe.wait_ge(*at("consts"))
            pe.wait_ge(*at("lambda_terms"))
            ps = open_bank(pe, XX, "lambda")
            pe.matmul(ps[:, 0:4], cst("ones", 0, P, DH), SM[0:DH, 0:4], start=True, stop=True) \
                .then_inc(*tick("squares_used", "lambda_sum"))
            modulation(0, 0)
            modulation(0, 1)
            modulation_turned(0, 0)
            sum_squares(("n1", 0), cst("ones"), KC, slice(0, T))
            modulation(0, 2)
            modulation_turned(0, 1)
            modulation(0, 3)
            modulation_turned(0, 2)
            modulation_turned(0, 3)

            for l in range(DEPTH):
                cs = cols(l)
                if l:
                    sum_squares(("n1", l), cst("ones"), KC, slice(0, T))

                def head_stats(c, l=l):
                    qc = cs if c < 4 else slice(0, T)
                    sum_squares(("qk", l, c), cst("blk"), 1, qc)
                    ps = open_bank(pe, XX, ("rot", l, c))
                    pe.wait_ge(*at(("qg", l, c)))
                    pe.matmul(ps[:, 0:S], cst("rot"), QG[:, c % 2, S:T], start=True, stop=True) \
                        .then_inc(*tick("rotated", ("rot", l, c)))

                for c in range(8):
                    qc = cs if c < 4 else slice(0, T)
                    by_feature(f"{'qk'[c // 4]}{c % 4}.{l}", ("h1", l), qc, qc.stop - qc.start)
                    if c:
                        head_stats(c - 1)
                by_token(f"v.{l}", ("h1", l), [0, P, 2 * P, 3 * P], 512)
                head_stats(7)
                for n in ("up0", "up1", "cb0", "ca0", "cb1", "ca1"):
                    by_feature(f"{n}.{l}", ("h1", l), cs, cs.stop - cs.start)

                us = units[l]

                def scores(i, l=l):
                    s, q, h = us[i]
                    nk = T if s else S
                    if i == 0:
                        for c in range(8):
                            pe.wait_ge(*at(("qkn", l, c)))
                    for c in range(2):
                        ps = open_bank(pe, MM, ("s", l, i, c))
                        r = slice(c * DH, c * DH + DH)
                        q0 = s * S + q * P
                        pe.matmul(ps[:, 0:nk], QKN[r, h, q0:q0 + P], QKN[r, 4 + h, 0:nk], start=True, stop=True) \
                            .then_inc(*tick("scores_done", ("s", l, i, c)))

                def turn_probs(i, l=l):
                    nk = T if us[i][0] else S
                    ps = open_bank(pe, XX, ("aT", l, i))
                    pe.wait_ge(*at(("a", l, i)))
                    transposes(ps, [AA[:, i % 2, j * P:(j + 1) * P] for j in range(nk // P)], ("aT", l, i))

                def values(i, l=l):
                    s, q, h = us[i]
                    nk = T if s else S
                    ps = open_bank(pe, XX, ("o", l, i))
                    if i == 0:
                        for t in range(4):
                            pe.wait_ge(*at(("vt", l, t)))
                    pe.wait_ge(*at(("aTs", l, i)))
                    for j in range(nk // P):
                        mm = pe.matmul(ps[:, 0:P], AT[:, i % 2, j * P:(j + 1) * P],
                                       VT[:, j, h * P:(h + 1) * P], start=(j == 0), stop=(j == nk // P - 1))
                    mm.then_inc(*tick("values_done", ("o", l, i)))

                pe.wait_ge(*at("pw"))
                for i in range(len(us) + 2):
                    if i < len(us):
                        scores(i)
                    if i < len(filler[l]):
                        modulation(*filler[l][i])
                    if 1 <= i <= len(filler[l]):
                        modulation_turned(*filler[l][i - 1])
                    if 1 <= i <= len(us):
                        turn_probs(i - 1)
                    if i >= 2:
                        values(i - 2)

                ncs = T if l == 0 else S
                for j in range(2):
                    ps = open_bank(pe, XX, ("pool", l, j))
                    pe.wait_ge(*at(("pl", l, j)))
                    pe.matmul(ps[:, 0:ncs], PW[:, 2 * l + j, :], PL[:, j, cs], start=True, stop=True) \
                        .then_inc(*tick("pooled", ("pool", l, j)))
                ps = open_bank(pe, XX, ("cmean", l))
                for j in range(2):
                    pe.wait_ge(*at(("cv", l, j)))
                    mm = pe.matmul(ps[:, 0:ncs], cst("ones"), CV[:, j, cs], start=(j == 0), stop=(j == 1))
                mm.then_inc(*tick("pooled", ("cmean", l)))
                sum_squares(("cvar", l), cst("ones"), 2, cs)
                for s, q in tiles[l]:
                    ps = open_bank(pe, XX, ("oT", l, s, q))
                    pe.wait_ge(*at(("on", l, s, q)))
                    transposes(ps, [ON[:, 2 * s + q, h * P:(h + 1) * P] for h in range(HEADS)], ("oT", l, s, q))
                for d in range(8):
                    by_feature(f"wo{d}.{l}", ("mixed", l), cs, ncs)
                sum_squares(("n2", l), cst("ones"), KC, cs)
                for j in range(FC):
                    by_feature(f"g{j}.{l}", ("h2", l), cs, ncs)
                    by_feature(f"u{j}.{l}", ("h2", l), cs, ncs)
                for d in range(8):
                    by_feature(f"fo{d}.{l}", ("hid", l), cs, ncs, (HIDH, HIDL))

            second_pe(pe, by_feature, by_token, sum_squares, transposes, product)

        @block.sync
        def _(sp):
            for s in range(NSLOT):
                if s >= RAW:
                    p = s - RAW
                    sp.wait_ge(*at(("lo", p)))
                sp.dma_start(RAWW[:, s % RAW, :], io["w"][s]).then_inc(*tick(f"landed{s % RAW}", ("landed", s), by=16))
            for kc in range(KC):
                sp.wait_ge(*at(("out", kc)))
            sp.dma_start(io["out"], XT[:, :, S:T]).then_inc(*tick("stored", "stored", by=16))
            sp.wait_ge(*at("stored"))

        @block.gpsimd
        def _(pool):
            done = [0]

            def upper_parts(until):
                while done[0] < until:
                    i = done[0]
                    pool.wait_ge(*at(("landed", i)))
                    if i >= SPLIT:
                        pool.wait_ge(*at(("slot", i - SPLIT)))
                    pool.tensor_scalar(WH[:, i % SPLIT, :], RAWW[:, i % RAW, :], 1.0, 0.0, ALU.mult, ALU.add) \
                        .then_inc(*tick("upper", ("hi", i)))
                    done[0] += 1

            for l in range(DEPTH):
                upper_parts(whole[f"ca1.{l}"])
                st = slice(0, 2) if l == 0 else slice(1, 2)
                L = S + 2 * UPAD
                for j in range(2):
                    pool.wait_ge(*at(("up", l, j)))
                    cur, w = UP[:, j, st, :], 1
                    for k in range(2 if j == 0 else 4):
                        ln = L - 2 * w + 1
                        rows = slice(0, P)
                        if (j, k) in ((0, 1), (1, 3)):
                            rows = slice(DH, P)
                        dst = WA[rows, k % 2, st, 0:ln]
                        link(pool, "pool_chain", pool.tensor_tensor(dst, cur[rows, :, 0:ln], cur[rows, :, w:w + ln], ALU.add))
                        cur = WA[:, k % 2, st, :]
                        w *= 2
                        if (j, k) in ((0, 0), (1, 2)):
                            g = 2 * j
                            half(pool, l, j, 0, WINDOWS[g], WA[0:DH, k % 2, st, :], st)
                    half(pool, l, j, 1, WINDOWS[2 * j + 1], WA[DH:P, (1 if j == 0 else 3) % 2, st, :], st)
            upper_parts(whole["vd"])
            pool.wait_ge(*at("rgws"))
            pool.wait_ge(*at("c2"))
            tril = cst("tril").unsqueeze(1).to_broadcast([P, 8, P])
            pool.tensor_tensor(WS, WS, tril, ALU.mult).then_inc(*tick("ws_masked", "ws_masked"))
            pool.wait_ge(*at("ws_masked"))
            upper_parts(NSLOT)

        @block.scalar
        def _(act):
            squares = [0]
            act.dma_start(PAR[:], io["par"]).then_inc(*tick("par_landed", "params", by=16))
            act.dma_start(CST[:], io["cst"][:, 0:NFIRST]).then_inc(*tick("cst_landed", "consts", by=16))
            act.dma_start(XT[:], io["x"]).then_inc(*tick("x_landed", "x_in", by=16))
            act.dma_start(PW[:].rearrange("p a b -> p (a b)"), io["pw"]).then_inc(*tick("pw_landed", "pw", by=16))

            def square(src, cs, **kw):
                q = squares[0]
                if q >= 2:
                    act.wait_ge(*at(("sq_used", q - 2)))
                squares[0] += 1
                return act.activation(SQ[:, q % 2, cs], src, ACT.Square, **kw).then_inc(*tick("squares_ready", ("sq", q)))

            def root(name, dst, n, mean, free_it=True):
                act.wait_ge(*at(("sum", name)))
                act.activation(dst[:, 0:n], bank(name)[:, 0:n], ACT.Sqrt, bias=SM[:, 8:9], scale=mean) \
                    .then_inc(*free(name, ("root", name)))

            def norm_squares(l, w, cs):
                for kc in range(KC):
                    for s in ((0, 1) if cs.start == 0 else (1,)):
                        if (w, l) == ("n1", 0):
                            act.wait_ge(*at("x_in"))
                        else:
                            act.wait_ge(*at(("x", "wo", l, kc, s) if w == "n2" else ("x", "fo", l - 1, kc, s)))
                    square(XT[:, kc, cs], cs)

            def norm_upper(l, w, which, cs, prev):
                act.wait_ge(*at(prev))
                for kc in range(KC):
                    for s in ((0, 1) if cs.start == 0 else (1,)):
                        sl = slice(s * S, s * S + S)
                        act.wait_ge(*at(("hn", w, l, kc, s)))
                        act.activation(AH[:, kc, sl], TF[:, kc % 2, sl], ACT.Identity,
                                       bias=MOD[:, l, 24 * which + kc, s:s + 1]) \
                            .then_inc(*tick("operand_upper", ("ah", w, l, kc, s)))

            act.wait_ge(*at("params"))
            act.activation(CT[:].rearrange("p k s -> p (k s)"), par("c", 0, 2 * KC), ACT.Silu) \
                .then_inc(*tick("conditions", "conditions"))
            act.wait_ge(*at("conditions"))
            act.activation(C4[:, :, 0:2], CT[:], ACT.Identity).then_inc(*tick("conditions", "c_upper"))
            act.wait_ge(*at("lambda_sum"))
            act.activation(SM[:, 4:8], bank("lambda")[:, 0:4], ACT.Exp).then_inc(*free("lambda", "lambda_exps"))
            act.wait_ge(*at("small"))

            turned_rows = []

            def modulation_rows(l, g):
                act.wait_ge(*at(("mm", f"mod{g}.{l}", 0)))
                if len(turned_rows) >= 2:
                    act.wait_ge(*at(("modT",) + turned_rows[-2]))
                turned_rows.append((l, g))
                act.activation(TF[0:4, g % 2, :], bank(f"mod{g}.{l}")[0:4, :], ACT.Copy) \
                    .then_inc(*free(f"mod{g}.{l}", ("mod_rows", l, g)))

            modulation_rows(0, 0)
            modulation_rows(0, 1)
            norm_squares(0, "n1", slice(0, T))
            root(("n1", 0), RS, T, 1.0 / D)
            modulation_rows(0, 2)
            modulation_rows(0, 3)
            for l in range(DEPTH):
                cs = cols(l)
                n_x = cs.stop - cs.start
                if l:
                    norm_squares(l, "n1", slice(0, T))
                    root(("n1", l), RS, T, 1.0 / D)
                norm_upper(l, "n1", 0, slice(0, T), "params" if l == 0 else ("mm", "u21.0", 0))

                def head_evac(c):
                    qc = cs if c < 4 else slice(0, T)
                    n = qc.stop - qc.start
                    name = f"{'qk'[c // 4]}{c % 4}.{l}"
                    act.wait_ge(*at(("mm", name, 0)))
                    square(bank(name)[:, 0:n], qc)
                    if c >= 2:
                        act.wait_ge(*at(("rot", l, c - 2)))
                        act.wait_ge(*at(("qgu", l, c - 2)))
                    g = SM[:, 12 + l:13 + l] if c < 4 else par("kg", l)
                    if l == 1 and c == 0:
                        act.wait_ge(*at(("mm", "fo7.0", 0)))
                    act.activation(QG[:, c % 2, qc], bank(name)[:, 0:n], ACT.Identity, scale=g) \
                        .then_inc(*free(name, ("qg", l, c)))

                def head_root(c):
                    n = n_x if c < 4 else T
                    if c:
                        act.wait_ge(*at(("rr", l, c - 1)))
                    root(("qk", l, c), RS, n, 1.0 / DH)

                for c in range(8):
                    head_evac(c)
                    if c:
                        head_root(c - 1)
                for t in range(4):
                    act.wait_ge(*at(("mm", f"v.{l}", t)))
                    act.activation(VT[:, t, :], bank((f"v.{l}", t))[:], ACT.Copy).then_inc(*free((f"v.{l}", t), ("vt", l, t)))
                head_root(7)
                st = slice(0, 2) if l == 0 else slice(1, 2)
                for j in range(2):
                    act.wait_ge(*at(("mm", f"up{j}.{l}", 0)))
                    if j == 0:
                        act.wait_ge(*at(("zeros", l)))
                    act.activation(UP[:, j, st, UPAD:UPAD + S], bank(f"up{j}.{l}")[:, 0:n_x].rearrange("p (s t) -> p s t", t=S), ACT.Copy) \
                        .then_inc(*free(f"up{j}.{l}", ("up", l, j)))
                for j in range(2):
                    act.wait_ge(*at(("mm", f"cb{j}.{l}", 0)))
                    act.activation(SGB[:, j, cs], bank(f"cb{j}.{l}")[:, 0:n_x], ACT.Sigmoid) \
                        .then_inc(*free(f"cb{j}.{l}", ("sgb", l, j)))

                us = units[l]

                def probs(i):
                    nk = T if us[i][0] else S
                    if i == 0:
                        act.wait_ge(*at(("cp", l, 1)))
                        act.wait_ge(*at(("pl", l, 1)))
                    for c in range(2):
                        act.wait_ge(*at(("nmax", l, i, c)))
                        if i >= 2:
                            act.wait_ge(*at(("a", l, i - 2)))
                        act.activation(PX[:, i % 2, c, 0:nk], bank(("s", l, i, c))[:, 0:nk], ACT.Exp,
                                       bias=SM[:, 16 + 2 * (i % 4) + c:17 + 2 * (i % 4) + c],
                                       accum_out=SM[:, 32 + 2 * i + c:33 + 2 * i + c]) \
                            .then_inc(*free(("s", l, i, c), ("p", l, i, c)))

                def turned(i):
                    nk = T if us[i][0] else S
                    act.wait_ge(*at(("aT", l, i)))
                    if i >= 2:
                        act.wait_ge(*at(("o", l, i - 2)))
                    act.activation(AT[:, i % 2, 0:nk], bank(("aT", l, i))[:, 0:nk], ACT.Copy) \
                        .then_inc(*free(("aT", l, i), ("aTs", l, i)))

                def output(i):
                    s, q, h = us[i]
                    act.wait_ge(*at(("o", l, i)))
                    act.wait_ge(*at(("ratio", l, i)))
                    o = ON[:, 2 * s + q, h * P:(h + 1) * P]
                    act.activation(o, bank(("o", l, i))[:, 0:P], ACT.Identity, scale=SM[:, 64 + i:65 + i]) \
                        .then_inc(*free(("o", l, i), ("orow", l, i)))
                    act.wait_ge(*at(("orow", l, i)))
                    act.activation(RS[:, 0:P], o, ACT.Square, accum_out=SM[:, 80 + i:81 + i]) \
                        .then_inc(*tick("output_squares", ("oss", l, i)))

                for i in range(len(us) + 2):
                    if i < len(us):
                        probs(i)
                    if i < len(filler[l]):
                        modulation_rows(*filler[l][i])
                    if 1 <= i <= len(us):
                        turned(i - 1)
                    if i >= 2:
                        output(i - 2)
                act.wait_ge(*at(("oss", l, len(us) - 1)))
                act.activation(SM[:, 96:96 + len(us)], SM[:, 80:80 + len(us)], ACT.Sqrt, bias=SM[:, 8:9], scale=1.0 / P) \
                    .then_inc(*tick("output_roots", ("oroot", l)))
                for j in range(2):
                    act.wait_ge(*at(("pool", l, j)))
                    act.activation(MIX[:, 4 + j, cs], bank(("pool", l, j))[:, 0:n_x], ACT.Identity, scale=par("ps", 2 * l + j)) \
                        .then_inc(*free(("pool", l, j), ("mix", l, 4 + j)))
                for j in range(2):
                    act.wait_ge(*at(("cd", l, j)))
                    square(CV[:, j, cs], cs)
                root(("cvar", l), RS, n_x, 1.0 / 256)
                for j in range(2):
                    act.wait_ge(*at(("cn", l, j)))
                    act.activation(MIX[:, 6 + j, cs], CV[:, j, cs], ACT.Silu, bias=par("lb2", 2 * l + j), scale=par("lg", 2 * l + j)) \
                        .then_inc(*tick("mixed_conv", ("mix", l, 6 + j)))
                for s, q in tiles[l]:
                    act.wait_ge(*at(("oT", l, s, q)))
                    c0 = s * S + q * P
                    act.activation(MIX[:, 0:4, c0:c0 + P], bank(("oT", l, s, q))[:].rearrange("p (h t) -> p h t", t=P),
                                   ACT.Identity, scale=SM[:, 14 + l:15 + l]) \
                        .then_inc(*free(("oT", l, s, q), ("mixo", l, s, q)))
                act.wait_ge(*at(("mm", f"ca1.{l}", 0)))
                act.wait_ge(*at(("mixo", l) + tiles[l][-1]))
                act.wait_ge(*at(("mix", l, 5)))
                act.wait_ge(*at(("mix", l, 7)))
                for kc in (4, 5, 6, 7, 0, 1, 2, 3):
                    act.activation(AH[:, kc, cs], MIX[:, kc, cs], ACT.Identity).then_inc(*tick("operand_upper", ("ahm", l, kc)))

                norm_squares(l, "n2", cs)
                act.wait_ge(*at(("lastrr", l)))
                root(("n2", l), RS, n_x, 1.0 / D)
                norm_upper(l, "n2", 1, cs, ("mm", f"wo7.{l}", 0))
                for j in range(FC):
                    act.wait_ge(*at(("mm", f"g{j}.{l}", 0)))
                    if j >= 2:
                        act.wait_ge(*at(("hf", l, j - 2)))
                    act.activation(SQ[:, j % 2, cs], bank(f"g{j}.{l}")[:, 0:n_x], ACT.Silu) \
                        .then_inc(*free(f"g{j}.{l}", ("gate", l, j)))
                    if j:
                        hidden_upper(act, l, j - 1, cs)
                hidden_upper(act, l, FC - 1, cs)
            second_act(act, square, root)

        @block.vector
        def _(dve):
            done = [0]

            def lower_parts(until):
                while done[0] < until:
                    i = done[0]
                    dve.wait_ge(*at(("hi", i)))
                    dve.tensor_tensor(WL[:, i % SPLIT, :], RAWW[:, i % RAW, :], WH[:, i % SPLIT, :].bitcast(F32), ALU.subtract) \
                        .then_inc(*tick("lower", ("lo", i)))
                    done[0] += 1

            def weights(name):
                prev = before.get(name)
                got = max(whole[prev] if prev else 0, whole[name] - 1)
                until = min(got + SPLIT, NSLOT)
                lower_parts(until)

            def L(ins):
                link(dve, "dve_chain", ins)

            for t in (CP, UP):
                L(dve.memset(t[:], 0.0))
            L(dve.memset(SM[:, 8:9], EPS))
            dve.wait_ge(*at("params"))
            dve.tensor_tensor(SM[0:DH, 0:4], par("la", 0, 4, DH), par("lb", 0, 4, DH), ALU.mult) \
                .then_inc(*tick("lambda_terms", "lambda_terms"))
            for l in range(DEPTH):
                init = 0.8 - 0.6 * math.exp(-0.3 * l)
                L(dve.tensor_scalar(SM[:, 12 + l:13 + l], par("qg", l), DH ** -0.5, None, ALU.mult))
                L(dve.tensor_scalar(SM[:, 14 + l:15 + l], par("sub", l), 1.0 - init, None, ALU.mult))
            dve.wait_ge(*at("c_upper"))
            dve.tensor_tensor(C4[:, :, 2:4], CT[:], C4[:, :, 0:2].bitcast(F32), ALU.subtract).then_inc(*tick("conditions_left", "c_left"))
            dve.wait_ge(*at("lambda_exps"))
            for l in range(DEPTH):
                init = 0.8 - 0.6 * math.exp(-0.3 * l)
                L(dve.tensor_tensor(SM[:, 10 + l:11 + l], SM[:, 5 + 2 * l:6 + 2 * l], SM[:, 4 + 2 * l:5 + 2 * l], ALU.subtract))
                ins = dve.tensor_scalar(SM[:, 10 + l:11 + l], SM[:, 10 + l:11 + l], -init, None, ALU.add)
                if l == 0:
                    L(ins)
                else:
                    ins.then_inc(*tick("small_ready", "small"))

            def modulation(l, g):
                dve.wait_ge(*at(("modT", l, g)))
                o = 4 * g
                bias = par("bmod", 48 * l + o, 4).unsqueeze(2).to_broadcast([P, 4, 2])
                dve.tensor_tensor(MOD[:, l, o:o + 4, :], bank(("modT", l, g))[:, 0:8].rearrange("p (a b) -> p a b", b=2),
                                  bias, ALU.add).then_inc(*free(("modT", l, g), ("mod", l, g)))
                dve.wait_ge(*at(("mod", l, g)))
                for w, n, oc in ((0, "n1", 8), (1, "n2", 32)):
                    if oc <= o < oc + 8:
                        gain = par(n, 8 * l + o - oc, 4).unsqueeze(2).to_broadcast([P, 4, 2])
                        L(dve.scalar_tensor_tensor(out=A1[:, l, w, o - oc:o - oc + 4, :], in0=MOD[:, l, o:o + 4, :], scalar=1.0,
                                                   in1=gain, op0=ALU.add, op1=ALU.mult))

            def reciprocal_root(name, n, *keys):
                dve.wait_ge(*at(("root", name)))
                dve.reciprocal(RR[:, 0:n], RS[:, 0:n]).then_inc(*tick("reciprocals", *keys))
                dve.wait_ge(*at(keys[0]))

            def norm(l, w, which, cs, fill, prev, name):
                for kc in range(KC):
                    for s in ((0, 1) if cs.start == 0 else (1,)):
                        sl = slice(s * S, s * S + S)
                        if kc >= 2:
                            dve.wait_ge(*at(("al", w, l, kc - 2, s)))
                        a = A1[:, l, which, kc, s:s + 1]
                        dve.scalar_tensor_tensor(out=TF[:, kc % 2, sl], in0=XT[:, kc, sl], scalar=a,
                                                 in1=RR[:, s * S - cs.start:s * S - cs.start + S], op0=ALU.mult, op1=ALU.mult) \
                            .then_inc(*tick("normed", ("hn", w, l, kc, s)))
                    if kc:
                        left(l, w, which, cs, fill, kc - 1)
                left(l, w, which, cs, fill, KC - 1)

            def left(l, w, which, cs, fill, kc):
                ss = (0, 1) if cs.start == 0 else (1,)
                for s in ss:
                    sl = slice(s * S, s * S + S)
                    dve.wait_ge(*at(("ah", w, l, kc, s)))
                    ins = dve.scalar_tensor_tensor(out=AL[:, kc, sl], in0=TF[:, kc % 2, sl],
                                                   scalar=MOD[:, l, 24 * which + kc, s:s + 1],
                                                   in1=AH[:, kc, sl].bitcast(F32), op0=ALU.add, op1=ALU.subtract)
                    ins.then_inc(*tick("operand_ready", ("al", w, l, kc, s), *([(fill, kc)] if s == 1 else [])))

            def residual(run, which, l, d, cs, tag):
                weights(run)
                dve.wait_ge(*at(("mm", run, 0)))
                ss = (0, 1) if cs.start == 0 else (1,)
                for s in ss:
                    sl = slice(s * S, s * S + S)
                    ins = dve.scalar_tensor_tensor(out=XT[:, d, sl], in0=bank(run)[:, sl.start - cs.start:sl.stop - cs.start],
                                                   scalar=MOD[:, l, which + d, s:s + 1], in1=XT[:, d, sl],
                                                   op0=ALU.mult, op1=ALU.add)
                    if s == 1:
                        ins.then_inc(*free(run, ("x", tag, l, d, 0), ("x", tag, l, d, 1)))
                    else:
                        L(ins)

            weights("mod0.0")
            weights("mod1.0")
            modulation(0, 0)
            weights("mod2.0")
            modulation(0, 1)
            weights("mod3.0")
            reciprocal_root(("n1", 0), T, ("rr1", 0))
            modulation(0, 2)
            modulation(0, 3)
            for l in range(DEPTH):
                cs = cols(l)
                n_x = cs.stop - cs.start
                if l:
                    reciprocal_root(("n1", l), T, ("rr1", l))
                norm(l, "n1", 0, slice(0, T), ("h1", l), None, None)
                weights(f"q0.{l}")

                def head(c):
                    n = n_x if c < 4 else T
                    off = S if n == S else 0
                    reciprocal_root(("qk", l, c), n, ("rr", l, c))
                    dve.wait_ge(*at(("qg", l, c)))
                    b, rot = c % 2, bank(("rot", l, c))
                    dve.wait_ge(*at(("rot", l, c)))
                    dve.tensor_tensor(TF[:, b, S:T], rot[:, 0:S], cst("sin"), ALU.mult) \
                        .then_inc(*free(("rot", l, c), ("rsin", l, c)))
                    L(dve.tensor_tensor(TF[:, b, 0:S], QG[:, b, S:T], cst("cos"), ALU.mult))
                    dve.wait_ge(*at(("rsin", l, c)))
                    L(dve.tensor_tensor(TF[:, b, S:T], TF[:, b, S:T], TF[:, b, 0:S], ALU.add))
                    if n == T:
                        L(dve.tensor_tensor(QKN[:, c, 0:S], QG[:, b, 0:S], RR[:, 0:S], ALU.mult))
                    dve.tensor_tensor(QKN[:, c, S:T], TF[:, b, S:T], RR[:, S - off:T - off], ALU.mult) \
                        .then_inc(*tick("heads_ready", ("qkn", l, c), ("qgu", l, c)))

                for c in range(8):
                    weights(f"{'qk'[c // 4]}{c % 4}.{l}")
                    if c:
                        head(c - 1)
                weights(f"v.{l}")
                head(7)
                for n in ("up0", "up1"):
                    weights(f"{n}.{l}")
                if l == 1:
                    L(dve.memset(CP[:], 0.0))
                    dve.memset(UP[:], 0.0).then_inc(*tick("zeroed", ("zeros", l)))
                else:
                    dve.memset(SM[:, 9:10], 0.0).then_inc(*tick("zeroed", ("zeros", l)))
                st = slice(0, 2) if l == 0 else slice(1, 2)
                for j in range(2):
                    weights(f"cb{j}.{l}")
                    weights(f"ca{j}.{l}")
                    dve.wait_ge(*at(("sgb", l, j)))
                    dve.wait_ge(*at(("mm", f"ca{j}.{l}", 0)))
                    dve.tensor_tensor(CP[:, j, st, PAD:PAD + S], bank(f"ca{j}.{l}")[:, 0:n_x].rearrange("p (s t) -> p s t", t=S),
                                      SGB[:, j, cs].rearrange("p (s t) -> p s t", t=S), ALU.mult) \
                        .then_inc(*free(f"ca{j}.{l}", ("cp", l, j)))

                us = units[l]
                taps = [(j, k) for j in range(2) for k in range(TAPS)]
                per = -(-len(taps) // len(us))

                def tap(j, k):
                    dst = CV[:, j, :].rearrange("p (s t) -> p s t", t=S)[:, st, :]
                    src = CP[:, j, st, k:k + S]
                    w = par("cw", (2 * l + j) * TAPS + k)
                    if k == 0:
                        dve.wait_ge(*at(("cp", l, j)))
                        ins = dve.tensor_scalar(dst, src, w, par("cb", 2 * l + j), ALU.mult, ALU.add)
                    else:
                        ins = dve.scalar_tensor_tensor(out=dst, in0=src, scalar=w, in1=dst, op0=ALU.mult, op1=ALU.add)
                    if k == TAPS - 1:
                        ins.then_inc(*tick("convolved", ("cv", l, j)))
                    else:
                        L(ins)

                def maxima(i):
                    nk = T if us[i][0] else S
                    for c in range(2):
                        dve.wait_ge(*at(("s", l, i, c)))
                        if i >= 4:
                            dve.wait_ge(*at(("p", l, i - 4, c)))
                        o = 16 + 2 * (i % 4) + c
                        dve.tensor_reduce(SM[:, o:o + 1], bank(("s", l, i, c))[:, 0:nk], AX.X, ALU.max, negate=True) \
                            .then_inc(*tick("maxima", ("nmax", l, i, c)))

                def combine(i):
                    nk = T if us[i][0] else S
                    dve.wait_ge(*at(("p", l, i, 0)))
                    dve.wait_ge(*at(("p", l, i, 1)))
                    s0, s1 = SM[:, 32 + 2 * i:33 + 2 * i], SM[:, 33 + 2 * i:34 + 2 * i]
                    L(dve.reciprocal(SM[:, 112:113], s1))
                    dve.reciprocal(SM[:, 64 + i:65 + i], s0).then_inc(*tick("ratios", ("ratio", l, i)))
                    L(dve.scalar_tensor_tensor(out=SM[:, 113:114], in0=s0, scalar=SM[:, 10 + l:11 + l], in1=SM[:, 112:113],
                                               op0=ALU.mult, op1=ALU.mult))
                    if i >= 2:
                        dve.wait_ge(*at(("aT", l, i - 2)))
                    dve.scalar_tensor_tensor(out=AA[:, i % 2, 0:nk], in0=PX[:, i % 2, 1, 0:nk], scalar=SM[:, 113:114],
                                             in1=PX[:, i % 2, 0, 0:nk], op0=ALU.mult, op1=ALU.add) \
                        .then_inc(*tick("differences", ("a", l, i)))

                maxima(0)
                def some_taps(n):
                    for _ in range(min(n, len(taps))):
                        tap(*taps.pop(0))

                for i in range(len(us)):
                    if i < len(filler[l]):
                        weights("mod{1}.{0}".format(*filler[l][i]))
                    some_taps(per)
                    if i + 1 < len(us):
                        maxima(i + 1)
                    combine(i)
                    if 1 <= i <= len(filler[l]):
                        modulation(*filler[l][i - 1])
                if len(filler[l]) == len(us):
                    modulation(*filler[l][-1])

                dve.wait_ge(*at(("cmean", l)))
                for j in range(2):
                    ins = dve.scalar_tensor_tensor(out=CV[:, j, cs], in0=bank(("cmean", l))[:, 0:n_x], scalar=-1.0 / 256,
                                                   in1=CV[:, j, cs], op0=ALU.mult, op1=ALU.add)
                    ins.then_inc(*(free(("cmean", l), ("cd", l, 1)) if j else tick("centred", ("cd", l, 0))))
                reciprocal_root(("cvar", l), n_x, ("lastrr", l))
                for j in range(2):
                    dve.wait_ge(*at(("cd", l, 1)))
                    dve.tensor_tensor(CV[:, j, cs], CV[:, j, cs], RR[:, 0:n_x], ALU.mult).then_inc(*tick("conv_normed", ("cn", l, j)))
                dve.wait_ge(*at(("oroot", l)))
                L(dve.reciprocal(SM[:, 96:96 + len(us)], SM[:, 96:96 + len(us)]))
                for n, (s, q) in enumerate(tiles[l]):
                    row = ON[:, 2 * s + q, :].rearrange("p (h e) -> p h e", e=P)
                    rs = SM[:, 96 + HEADS * n:100 + HEADS * n].unsqueeze(2).to_broadcast([P, HEADS, P])
                    dve.tensor_tensor(row, row, rs, ALU.mult).then_inc(*tick("rows_normed", ("on", l, s, q)))
                weights(f"wo0.{l}")
                for kc in (4, 5, 6, 7, 0, 1, 2, 3):
                    dve.wait_ge(*at(("ahm", l, kc)))
                    dve.tensor_tensor(AL[:, kc, cs], MIX[:, kc, cs], AH[:, kc, cs].bitcast(F32), ALU.subtract) \
                        .then_inc(*tick("operand_ready", (("mixed", l), kc)))

                for d in range(8):
                    residual(f"wo{d}.{l}", 16, l, d, cs, "wo")
                weights(f"g0.{l}")
                reciprocal_root(("n2", l), n_x, ("rr2", l))
                norm(l, "n2", 1, cs, ("h2", l), None, None)
                for j in range(FC):
                    weights(f"g{j}.{l}")
                    weights(f"u{j}.{l}")
                    dve.wait_ge(*at(("gate", l, j)))
                    dve.wait_ge(*at(("mm", f"u{j}.{l}", 0)))
                    if j >= 2:
                        dve.wait_ge(*at((("hid", l), j - 2)))
                    dve.tensor_tensor(TF[:, j % 2, cs], bank(f"u{j}.{l}")[:, 0:n_x], SQ[:, j % 2, cs], ALU.mult) \
                        .then_inc(*free(f"u{j}.{l}", ("hf", l, j)))
                    if j:
                        hidden_left(l, j - 1, cs)
                hidden_left(l, FC - 1, cs)
                for d in range(8):
                    residual(f"fo{d}.{l}", 40, l, d, cs, "fo")
            second_dve(dve, weights, L, reciprocal_root)

        return counts.found


def arrays(i):
    xt = np.concatenate([i["ctx"][0], i["x"][0]], axis=0).T.reshape(KC, P, T).transpose(1, 0, 2)
    return {
        "x": np.ascontiguousarray(xt),
        "w": weight_stream(i["w_mod"], i["w_in"], i["w_out"], i["w_ffn_in"], i["w_ffn_out"], i["w_in_2"],
                           i["w_branch_2"], i["w_out_2"]),
        "par": parameter_columns(i),
        "cst": shape_constants(),
        "pw": np.concatenate([block_diagonal(i["pool_w"][l]) for l in range(DEPTH)], axis=1).reshape(P, -1),
        "extra": extra_weights(i),
    }


def launchable(bacc, laid_out, known):
    nc = bacc.Bacc("TRN2", target_bir_lowering=False, num_devices=1)
    io = {n: nc.dram_tensor(f"in_{n}_dram", v.shape, F32, kind="ExternalInput").ap() for n, v in laid_out.items()}
    io["out"] = nc.dram_tensor("out_dram", (P, KC, S), F32, kind="ExternalOutput").ap()
    return nc, program(nc, io, known)


def kernel(**inputs):
    import concourse.bacc as bacc
    from concourse.bass_utils import run_bass_kernel_spmd

    laid_out = arrays({k: np.asarray(v) for k, v in inputs.items()})
    _, known = launchable(bacc, laid_out, {})
    nc, _ = launchable(bacc, laid_out, known)
    r = run_bass_kernel_spmd(nc, [{f"in_{n}_dram": v for n, v in laid_out.items()}], core_ids=[0])
    return r.results[0]["out_dram"].transpose(2, 1, 0).reshape(1, S, D)
```
